# Optimizing a Trainium2 kernel written in Bass

```python
import math
import jax, jax.numpy as jnp
from jax import lax
import numpy as np

D_MODEL = 2048
BATCH = 1
SEQ = 256
DEPTH = 2

D_MIX = D_MODEL
HEAD_DIM = 128
N_HEADS_A = 8
N_HEADS_B = 8
D_A = N_HEADS_A * HEAD_DIM
D_B = N_HEADS_B * HEAD_DIM
IDX_HEADS = 16
IDX_DIM = 64
TOPK_MAX = 256
Q_BLOCK = 128
RET_CHUNK = 128
N_BUCKETS = 32
MAX_EXACT = 16
MAX_DISTANCE = 128
ROPE_BASE = 10000.0
EPS = 1e-6
IN_SIZES = (D_A, HEAD_DIM, HEAD_DIM, D_A, IDX_HEADS * IDX_DIM, IDX_DIM, IDX_HEADS, D_B, D_B, D_B, D_B)
N_IN = 2 * D_A + 2 * HEAD_DIM + IDX_HEADS * IDX_DIM + IDX_DIM + IDX_HEADS + 4 * D_B


def rmsnorm(x, g):
    xf = x.astype(jnp.float32)
    y = xf * lax.rsqrt(jnp.mean(xf * xf, axis=-1, keepdims=True) + EPS)
    return (y * g.astype(jnp.float32)).astype(x.dtype)

def head_groupnorm(x, g):
    xf = x.astype(jnp.float32)
    mu = jnp.mean(xf, axis=-1, keepdims=True)
    var = jnp.mean(jnp.square(xf - mu), axis=-1, keepdims=True)
    y = (xf - mu) * lax.rsqrt(var + EPS)
    B, S, H, D = x.shape
    return (y.reshape(B, S, H * D) * g.astype(jnp.float32)).astype(x.dtype)

def rotary(x, pos):
    half = x.shape[-1] // 2
    inv = ROPE_BASE ** (-jnp.arange(half, dtype=jnp.float32) / half)
    ang = pos.astype(jnp.float32)[..., None] * inv
    cos = jnp.cos(ang)[:, :, None, :]
    sin = jnp.sin(ang)[:, :, None, :]
    xf = x.astype(jnp.float32)
    x1, x2 = xf[..., :half], xf[..., half:]
    return jnp.concatenate([x1 * cos - x2 * sin, x1 * sin + x2 * cos], axis=-1).astype(x.dtype)

def t5_bucket(rel):
    rel = jnp.maximum(rel, 0)
    relf = jnp.maximum(rel, 1).astype(jnp.float32)
    large = MAX_EXACT + (jnp.log(relf / MAX_EXACT) / math.log(MAX_DISTANCE / MAX_EXACT)
                         * (N_BUCKETS - MAX_EXACT)).astype(jnp.int32)
    large = jnp.minimum(large, N_BUCKETS - 1)
    return jnp.where(rel < MAX_EXACT, rel, large)

def sparse_attention(q, k, v, q_idx, k_idx, w_idx, pos, rel_bias):
    B, S, H, Dh = q.shape
    n_blk = S // Q_BLOCK
    top_k = min(TOPK_MAX, S // 4)
    scale = HEAD_DIM ** -0.5
    key_pos = jnp.arange(S)

    def block(xs):
        qb, qib, wb, pb, start = xs
        t = start + jnp.arange(Q_BLOCK)
        dots = jnp.einsum('bqhd,bsd->bqhs', qib, k_idx).astype(jnp.float32)
        I = jnp.einsum('bqh,bqhs->bqs', wb.astype(jnp.float32), jax.nn.relu(dots))
        causal = key_pos[None, :] <= t[:, None]
        I = jnp.where(causal[None], I, -jnp.inf)
        _, sel = lax.top_k(I, top_k)
        valid = sel <= t[None, :, None]
        ks = jax.vmap(lambda kb, ib: kb[ib])(k, sel)
        vs = jax.vmap(lambda vb, ib: vb[ib])(v, sel)
        ps = jax.vmap(lambda pb_, ib: pb_[ib])(pos, sel)
        bias = rel_bias[t5_bucket(pb[:, :, None] - ps)]
        bias = jnp.moveaxis(bias, -1, 2).astype(jnp.float32)
        logits = jnp.einsum('bqhd,bqkd->bqhk', qb, ks).astype(jnp.float32) * scale + bias
        logits = jnp.where(valid[:, :, None, :], logits, -jnp.inf)
        p = jax.nn.softmax(logits, axis=-1).astype(v.dtype)
        return jnp.einsum('bqhk,bqkd->bqhd', p, vs)

    def to_blocks(a):
        return a.reshape((B, n_blk, Q_BLOCK) + a.shape[2:]).swapaxes(0, 1)

    xs = (to_blocks(q), to_blocks(q_idx), to_blocks(w_idx), to_blocks(pos),
          jnp.arange(n_blk) * Q_BLOCK)
    out = lax.map(block, xs)
    return out.swapaxes(0, 1).reshape(B, S, H, Dh)

def retention(q, k, v):
    B, S, H, D = q.shape
    C = RET_CHUNK
    nC = S // C
    log_g = jnp.log1p(-jnp.exp2(-5.0 - jnp.arange(H, dtype=jnp.float32)))
    i = jnp.arange(C, dtype=jnp.float32)
    diff = i[:, None] - i[None, :]
    dmask = jnp.where(diff >= 0, jnp.exp(log_g[:, None, None] * jnp.maximum(diff, 0.0)), 0.0)
    qc = q.astype(jnp.float32).reshape(B, nC, C, H, D)
    kc = k.astype(jnp.float32).reshape(B, nC, C, H, D)
    vc = v.astype(jnp.float32).reshape(B, nC, C, H, D)
    s_in = jnp.einsum('bnihd,bnjhd->bnhij', qc, kc) * dmask
    intra = jnp.einsum('bnhij,bnjhd->bnihd', s_in, vc)
    zeta = jnp.exp(log_g[None, :] * (C - 1.0 - i)[:, None])
    u = jnp.einsum('bnjhd,bnjhe->bnhde', kc * zeta[None, None, :, :, None], vc)
    g_chunk = jnp.exp(log_g * C)[None, :, None, None]

    def step(R, u_n):
        return g_chunk * R + u_n, R

    _, R_prev = lax.scan(step, jnp.zeros((B, H, D, D), jnp.float32), u.swapaxes(0, 1))
    R_prev = R_prev.swapaxes(0, 1)
    xi = jnp.exp(log_g[None, :] * (i + 1.0)[:, None])
    cross = jnp.einsum('bnihd,bnhde->bnihe', qc, R_prev) * xi[None, None, :, :, None]
    return (intra + cross).reshape(B, S, H, D)

def first_inputs(seed: int = 0) -> dict:
    key = jax.random.key(seed)
    ks = jax.random.split(key, 12)
    f32 = jnp.float32
    x = jax.random.normal(ks[0], (BATCH, SEQ, D_MODEL), f32)
    c = jax.random.normal(ks[1], (BATCH, D_MODEL), f32)
    positions = jnp.broadcast_to(jnp.arange(SEQ, dtype=jnp.int32)[None, :], (BATCH, SEQ))
    rel_bias = 0.5 * jax.random.normal(ks[2], (N_BUCKETS, N_HEADS_A), f32)
    norm_gain = 1.0 + 0.05 * jax.random.normal(ks[3], (DEPTH, D_MODEL), f32)
    w_mod = 0.5 * D_MODEL ** -0.5 * jax.random.normal(ks[4], (DEPTH, D_MODEL, 3 * D_MODEL), f32)
    b_mod = 0.02 * jax.random.normal(ks[5], (DEPTH, 3 * D_MODEL), f32)
    w_in = D_MODEL ** -0.5 * jax.random.normal(ks[6], (DEPTH, D_MODEL, N_IN), f32)
    q_norm_gain = 1.0 + 0.05 * jax.random.normal(ks[7], (DEPTH, HEAD_DIM), f32)
    k_norm_gain = 1.0 + 0.05 * jax.random.normal(ks[8], (DEPTH, HEAD_DIM), f32)
    ret_norm_gain = 1.0 + 0.05 * jax.random.normal(ks[9], (DEPTH, D_B), f32)
    w_out = D_MIX ** -0.5 * jax.random.normal(ks[10], (DEPTH, D_MIX, D_MODEL), f32)
    return {"x": x, "c": c, "positions": positions, "rel_bias": rel_bias,
            "norm_gain": norm_gain, "w_mod": w_mod, "b_mod": b_mod, "w_in": w_in,
            "q_norm_gain": q_norm_gain, "k_norm_gain": k_norm_gain,
            "ret_norm_gain": ret_norm_gain, "w_out": w_out}

def first_block(x, c, positions, rel_bias, norm_gain, w_mod, b_mod, w_in,
              q_norm_gain, k_norm_gain, ret_norm_gain, w_out):
    B, S, _ = x.shape
    split_points = [int(p) for p in np.cumsum(IN_SIZES)[:-1]]
    c_act = jax.nn.silu(c)
    for l in range(DEPTH):
        mod = c_act @ w_mod[l] + b_mod[l]
        shift, scale, gate = jnp.split(mod, 3, axis=-1)
        h = rmsnorm(x, norm_gain[l]) * (1.0 + scale[:, None, :]) + shift[:, None, :]
        proj = h @ w_in[l]
        q_a, k_a, v_a, g_a, q_i, k_i, w_i, q_b, k_b, v_b, g_b = jnp.split(proj, split_points, axis=-1)
        q_a = rmsnorm(q_a.reshape(B, S, N_HEADS_A, HEAD_DIM), q_norm_gain[l])
        k_a = rmsnorm(k_a, k_norm_gain[l])
        att = sparse_attention(q_a, k_a, v_a, q_i.reshape(B, S, IDX_HEADS, IDX_DIM), k_i, w_i,
                               positions, rel_bias)
        y_a = att.reshape(B, S, D_A) * jax.nn.silu(g_a)
        q_b = rotary(q_b.reshape(B, S, N_HEADS_B, HEAD_DIM), positions)
        k_b = rotary(k_b.reshape(B, S, N_HEADS_B, HEAD_DIM), positions) * (HEAD_DIM ** -0.5)
        ret = retention(q_b, k_b, v_b.reshape(B, S, N_HEADS_B, HEAD_DIM))
        y_b = head_groupnorm(ret, ret_norm_gain[l]).astype(x.dtype) * jax.nn.silu(g_b)
        y = jnp.concatenate([y_a, y_b], axis=-1) @ w_out[l]
        x = x + gate[:, None, :] * y
    return x


DEPTH_2 = 1

CHUNK = 64
N_META = 16
SB_HEADS = 8
FOX_HEADS = 8
SB_WIDTH = SB_HEADS * HEAD_DIM
FOX_WIDTH = FOX_HEADS * HEAD_DIM
MIX_WIDTH = SB_WIDTH + FOX_WIDTH
C_IN = 3 * SB_WIDTH + 4 * FOX_WIDTH + FOX_HEADS
PEER_HEADS = 8
PEER_TOPK = 16
N_KEYS = 128
N_EXPERTS = N_KEYS * N_KEYS
D_KEY = 256
PEER_BLOCK = 128


def rms_norm(x, gain):
    xf = x.astype(jnp.float32)
    y = xf * lax.rsqrt(jnp.mean(xf * xf, axis=-1, keepdims=True) + EPS)
    return y.astype(x.dtype) * gain

def to_query_blocks(a):
    b, l = a.shape[:2]
    return jnp.moveaxis(a.reshape((b, l // Q_BLOCK, Q_BLOCK) + a.shape[2:]), 1, 0)

def from_query_blocks(a):
    a = jnp.moveaxis(a, 0, 1)
    b, nb, qb = a.shape[:3]
    return a.reshape(b, nb * qb, -1)

def stick_breaking_attention(q, k, v):
    L = k.shape[1]
    k_pos = jnp.arange(L)
    scale = 1.0 / math.sqrt(HEAD_DIM)
    starts = jnp.arange(L // Q_BLOCK, dtype=jnp.int32) * Q_BLOCK

    def block(args):
        qb, start = args
        q_pos = start + jnp.arange(Q_BLOCK)
        z = jnp.einsum('bqhd,bkhd->bhqk', qb, k).astype(jnp.float32) * scale
        visible = k_pos[None, :] < q_pos[:, None]
        log_1mb = jnp.where(visible, jax.nn.log_sigmoid(-z), 0.0)
        after = lax.cumsum(log_1mb, axis=3, reverse=True) - log_1mb
        w = jnp.where(visible, jnp.exp(jax.nn.log_sigmoid(z) + after), 0.0)
        return jnp.einsum('bhqk,bkhd->bqhd', w.astype(v.dtype), v)

    out = lax.map(block, (to_query_blocks(q), starts))
    return from_query_blocks(out)

def forgetting_attention(q, k, v, log_f):
    L = k.shape[1]
    k_pos = jnp.arange(L)
    scale = 1.0 / math.sqrt(HEAD_DIM)
    cum_f = lax.cumsum(log_f, axis=1)
    cum_f_k = jnp.transpose(cum_f, (0, 2, 1))
    starts = jnp.arange(L // Q_BLOCK, dtype=jnp.int32) * Q_BLOCK

    def block(args):
        qb, fq, start = args
        q_pos = start + jnp.arange(Q_BLOCK)
        z = jnp.einsum('bqhd,bkhd->bhqk', qb, k).astype(jnp.float32) * scale
        logits = z + jnp.transpose(fq, (0, 2, 1))[..., None] - cum_f_k[:, :, None, :]
        visible = k_pos[None, :] <= q_pos[:, None]
        p = jax.nn.softmax(jnp.where(visible, logits, -jnp.inf), axis=-1)
        return jnp.einsum('bhqk,bkhd->bqhd', p.astype(v.dtype), v)

    out = lax.map(block, (to_query_blocks(q), to_query_blocks(cum_f), starts))
    return from_query_blocks(out)

def mixer_sublayer(h, w_in, b_forget, fox_q_gain, fox_k_gain, sb_out_gain, fox_out_gain, w_out):
    B, L, _ = h.shape
    proj = h @ w_in
    s3 = 3 * SB_WIDTH
    sb_q, sb_k, sb_v, fq, fk, fv, fgate, flogit = jnp.split(
        proj,
        [SB_WIDTH, 2 * SB_WIDTH, s3, s3 + FOX_WIDTH, s3 + 2 * FOX_WIDTH,
         s3 + 3 * FOX_WIDTH, s3 + 4 * FOX_WIDTH],
        axis=-1)

    def heads(a, n):
        return a.reshape(B, L, n, HEAD_DIM)

    sb = stick_breaking_attention(heads(sb_q, SB_HEADS), heads(sb_k, SB_HEADS), heads(sb_v, SB_HEADS))
    log_f = jax.nn.log_sigmoid((flogit + b_forget).astype(jnp.float32))
    fox = forgetting_attention(rms_norm(heads(fq, FOX_HEADS), fox_q_gain),
                               rms_norm(heads(fk, FOX_HEADS), fox_k_gain),
                               heads(fv, FOX_HEADS), log_f)
    merged = jnp.concatenate(
        [rms_norm(sb, sb_out_gain),
         rms_norm(fox, fox_out_gain) * jax.nn.sigmoid(fgate)], axis=-1)
    return merged @ w_out

def peer_sublayer(h, w_query, sub_keys, u, v):
    B, L, D = h.shape
    blocks = h.reshape(-1, PEER_BLOCK, D)

    def block(hb):
        q = (hb @ w_query).reshape(PEER_BLOCK, PEER_HEADS, 2, D_KEY // 2)
        s = jnp.einsum('thpc,hpnc->thpn', q, sub_keys).astype(jnp.float32)
        top_s, top_i = lax.top_k(s, PEER_TOPK)
        cand_s = (top_s[:, :, 0, :, None] + top_s[:, :, 1, None, :]).reshape(PEER_BLOCK, PEER_HEADS, -1)
        cand_i = (top_i[:, :, 0, :, None] * N_KEYS + top_i[:, :, 1, None, :]).reshape(PEER_BLOCK, PEER_HEADS, -1)
        best_s, best_j = lax.top_k(cand_s, PEER_TOPK)
        idx = jnp.take_along_axis(cand_i, best_j, axis=-1)
        g = jax.nn.softmax(best_s, axis=-1)
        u_sel = jnp.take(u, idx, axis=0)
        a = jax.nn.gelu(jnp.einsum('thkd,td->thk', u_sel, hb), approximate=False)
        v_sel = jnp.take(v, idx, axis=0)
        return jnp.einsum('thk,thkd->td', (g * a).astype(hb.dtype), v_sel)

    return lax.map(block, blocks).reshape(B, L, D)

def second_inputs(seed: int = 0) -> dict:
    key = jax.random.key(seed)
    ks = jax.random.split(key, 15)
    f32 = jnp.float32
    nrm = lambda k, shape, s: jax.random.normal(k, shape, f32) * s
    gain = lambda k, shape: 1.0 + 0.02 * jax.random.normal(k, shape, f32)
    return {
        "x": nrm(ks[0], (BATCH, SEQ, D_MODEL), 1.0),
        "meta_tokens": nrm(ks[1], (N_META, D_MODEL), 1.0),
        "norm_mix": gain(ks[2], (DEPTH_2, D_MODEL)),
        "w_in": nrm(ks[3], (DEPTH_2, D_MODEL, C_IN), D_MODEL ** -0.5),
        "b_forget": jax.random.uniform(ks[4], (DEPTH_2, FOX_HEADS), f32, 1.0, 4.0),
        "fox_q_gain": gain(ks[5], (DEPTH_2, HEAD_DIM)),
        "fox_k_gain": gain(ks[6], (DEPTH_2, HEAD_DIM)),
        "sb_out_gain": gain(ks[7], (DEPTH_2, SB_WIDTH)),
        "fox_out_gain": gain(ks[8], (DEPTH_2, FOX_WIDTH)),
        "w_out": nrm(ks[9], (DEPTH_2, MIX_WIDTH, D_MODEL), MIX_WIDTH ** -0.5),
        "norm_ffn": gain(ks[10], (DEPTH_2, D_MODEL)),
        "peer_w_query": nrm(ks[11], (DEPTH_2, D_MODEL, PEER_HEADS * D_KEY), D_MODEL ** -0.5),
        "peer_sub_keys": nrm(ks[12], (DEPTH_2, PEER_HEADS, 2, N_KEYS, D_KEY // 2), (D_KEY // 2) ** -0.5),
        "peer_u": nrm(ks[13], (DEPTH_2, N_EXPERTS, D_MODEL), D_MODEL ** -0.5),
        "peer_v": nrm(ks[14], (DEPTH_2, N_EXPERTS, D_MODEL), PEER_HEADS ** -0.5),
    }

def second_block(x, meta_tokens, norm_mix, w_in, b_forget, fox_q_gain, fox_k_gain,
              sb_out_gain, fox_out_gain, w_out, norm_ffn, peer_w_query, peer_sub_keys,
              peer_u, peer_v):
    B, S, D = x.shape
    l_pad = ((S + N_META + Q_BLOCK - 1) // Q_BLOCK) * Q_BLOCK
    meta = jnp.broadcast_to(meta_tokens[None].astype(x.dtype), (B, N_META, D))
    pad = jnp.zeros((B, l_pad - S - N_META, D), x.dtype)
    h = jnp.concatenate([meta, x, pad], axis=1)
    for l in range(DEPTH_2):
        h = h + mixer_sublayer(rms_norm(h, norm_mix[l]), w_in[l], b_forget[l],
                               fox_q_gain[l], fox_k_gain[l], sb_out_gain[l],
                               fox_out_gain[l], w_out[l])
        h = h + peer_sublayer(rms_norm(h, norm_ffn[l]), peer_w_query[l],
                              peer_sub_keys[l], peer_u[l], peer_v[l])
    return h[:, N_META:N_META + S]


def setup_inputs(seed=0):
    out = dict(first_inputs(seed))
    for name, value in second_inputs(seed + 1).items():
        if name != "x":
            out[name + "_2"] = value
    return out


def reference(
    x, c, positions, rel_bias, norm_gain, w_mod, b_mod, w_in, q_norm_gain, k_norm_gain,
    ret_norm_gain, w_out, meta_tokens_2, norm_mix_2, w_in_2, b_forget_2, fox_q_gain_2,
    fox_k_gain_2, sb_out_gain_2, fox_out_gain_2, w_out_2, norm_ffn_2, peer_w_query_2,
    peer_sub_keys_2, peer_u_2, peer_v_2,
):
    x = first_block(
        x, c, positions, rel_bias, norm_gain, w_mod, b_mod, w_in, q_norm_gain, k_norm_gain,
        ret_norm_gain, w_out,
    )
    return second_block(
        x, meta_tokens_2, norm_mix_2, w_in_2, b_forget_2, fox_q_gain_2, fox_k_gain_2,
        sb_out_gain_2, fox_out_gain_2, w_out_2, norm_ffn_2, peer_w_query_2, peer_sub_keys_2,
        peer_u_2, peer_v_2,
    )


_drawn_inputs = setup_inputs


def setup_inputs(seed=0):
    import zlib

    import numpy as np

    out = dict(_drawn_inputs(seed))
    spreads = {}
    factors = {'q_norm_gain': 6.737,
     'k_norm_gain': 6.798,
     'ret_norm_gain': 2.79,
     'fox_q_gain_2': 4.65,
     'fox_k_gain_2': 4.994,
     'sb_out_gain_2': 8.072,
     'fox_out_gain_2': 13.626,
     'norm_ffn_2': 7.933}
    for name, (base, spread) in spreads.items():
        noise = np.random.default_rng([zlib.crc32(name.encode()), seed]).standard_normal(out[name].shape)
        drawn = base * np.exp(spread * noise) if base else spread * noise
        out[name] = __import__('jax').numpy.asarray(drawn.astype(out[name].dtype))
    for name, factor in factors.items():
        out[name] = (out[name] * factor).astype(out[name].dtype)
    return out
```

```python
from contextlib import ExitStack

import numpy as np

import concourse.bass as bass
from concourse import mybir

ALU = mybir.AluOpType
ACT = mybir.ActivationFunctionType
F32 = mybir.dt.float32
I32 = mybir.dt.int32
U32 = mybir.dt.uint32
AX = mybir.AxisListType.X

D = 2048
NK = 16
EPS = 1e-6
NEGV = -1.0e30
TAKEN = -3.0e38
SC = 128.0 ** -0.5

QA, KA, VA, GA, QI, KI, WI, QB, KB, VB, GB = (0, 1024, 1152, 1280, 2304, 3328, 3392, 3408, 4432, 5456, 6480)
NIN = 7504
SQ, SK, SV, FQ, FK, FV, FG, FL = (0, 1024, 2048, 3072, 4096, 5120, 6144, 7168)
CIN = 7176
MSK, MSV, MFK, MFV, MFL = (0, 1024, 2048, 3072, 4096)

ID, ONE, TRL, TRU, NTT, SM, NSM, INV, NCW = (0, 128, 256, 384, 512, 640, 768, 896, 1104)
ROWS1 = [("c", 16), ("norm_gain", 32), ("norm_mix_2", 16), ("q_norm_gain", 2), ("k_norm_gain", 2),
         ("fox_q_gain_2", 1), ("fox_k_gain_2", 1), ("ret_norm_gain", 16), ("sb_out_gain_2", 8),
         ("fox_out_gain_2", 8)]


def constants():
    i = np.arange(128)
    cw = np.zeros((128, NCW), np.float32)
    cw[:, ID:ID + 128] = np.eye(128)
    cw[:, ONE:ONE + 128] = 1.0
    cw[:, TRL:TRL + 128] = i[:, None] >= i[None, :]
    cw[:, TRU:TRU + 128] = i[:, None] <= i[None, :]
    cw[:, NTT:NTT + 128] = np.where(i[None, :] > i[:, None], NEGV, 0.0)
    cw[:, SM:SM + 128] = i[None, :] > i[:, None]
    cw[:, NSM:NSM + 128] = np.where(i[None, :] > i[:, None], 0.0, NEGV)
    inv = np.float32(10000.0) ** (-np.arange(64, dtype=np.float32) / np.float32(64))
    cw[:, INV:INV + 64] = inv.astype(np.float32)[None, :]
    cw[:, INV + 64:INV + 80] = np.arange(16)[None, :]
    lg = np.log1p(-np.exp2(-5.0 - np.arange(8)))
    j, t = np.arange(256)[:, None], np.arange(256)[None, :]
    dm = np.zeros((128, 8, 384), np.float32)
    for h in range(8):
        full = np.where(t >= j, np.exp(lg[h] * np.maximum(t - j, 0)), 0.0)
        dm[:, h, 0:256] = full[0:128]
        dm[:, h, 256:384] = full[128:256, 128:256]
    return cw, dm


class Lane:

    def __init__(self, sem):
        self.sem, self.n, self.q, self.seen = sem, 0, [], {}

    def now(self):
        return (self.sem, self.n)

    def wait(self, *marks):
        for m in marks:
            if m is None or m[1] == 0 or self.seen.get(id(m[0]), 0) >= m[1]:
                continue
            self.seen[id(m[0])] = m[1]
            self.q.append(lambda e, m=m: e.wait_ge(m[0], m[1]))

    def do(self, fn, *marks):
        self.wait(*marks)
        self.n += 1
        self.q.append(lambda e, fn=fn: fn(e).then_inc(self.sem, 1))
        return self.now()

    def then(self, fn, *marks):
        return self.do(fn, *marks, self.now())

    def plain(self, fn, *marks):
        self.wait(*marks)
        self.q.append(fn)

    def dma(self, sem, cnt, fn, *marks):
        self.wait(*marks)
        cnt[0] += 16
        self.q.append(lambda e, fn=fn: fn(e).then_inc(sem, 16))
        return (sem, cnt[0])


def mixer_peer_program(nc, I, out):
    with ExitStack() as ctx:
        def sb(name, shape, dt=F32):
            return ctx.enter_context(nc.sbuf_tensor(name, shape, dt))

        def sem(name):
            return ctx.enter_context(nc.semaphore(name))

        V, A, T, G, S_ = (Lane(sem("l_" + n)) for n in ("v", "a", "t", "g", "s"))

        NS = 7
        x = sb("x", [128, 2, D])
        hT = sb("hT", [128, NK, 272])
        P = sb("P", [128, 2, NIN])
        ring = sb("ring", [128, NS, 2048])
        U = sb("U", [128, 4608])
        TAB = sb("TAB", [128, 4224])
        S = sb("S", [128, 2560])
        CW = sb("CW", [128, NCW])
        cols = sb("cols", [128, 102])
        bcol = sb("bcol", [128, 96])
        cact = sb("cact", [128, 16])
        cs = sb("cs", [128, 2, 2, 64])
        mcol = sb("mcol", [128, 48])
        KIT = sb("KIT", [128, 2, 256])
        KAT = sb("KAT", [128, 256])
        IW = sb("IW", [128, 256])
        NEG = sb("NEG", [128, 384])
        sm = sb("sm", [128, 160])
        lf = sb("lf", [128, 3, 8])
        fcol = sb("fcol", [128, 2, 8])
        TA = TAB[:, 0:2048].rearrange("p (h n) -> p h n", h=8)
        TB = TAB[:, 2048:4224].rearrange("p (h n) -> p h n", h=8)
        ident = CW[:, ID:ID + 128]
        ones = CW[:, ONE:ONE + 128]

        pp = [ctx.enter_context(nc.psum_tensor(f"pp{i}", [128, 512], F32)) for i in range(4)]
        tp = [ctx.enter_context(nc.psum_tensor(f"tp{i}", [128, 1024], F32)) for i in range(2)]
        pp_free = [None] * 4
        tp_free = [[], []]
        tpn = [0]

        def pair():
            i = tpn[0] % 2
            tpn[0] += 1
            T.wait(*tp_free[i])
            return tp[i], i

        r_sem = [sem(f"s_r{i}") for i in range(NS)]
        r_cnt = [[0] for _ in range(NS)]
        r_free = [[] for _ in range(NS)]
        rn = [0]
        s_c, s_cn = sem("s_c"), [0]
        s_d, s_dn = [sem("s_d0"), sem("s_d1")], [[0], [0]]
        s_m, s_mn = [sem(f"s_m{j}") for j in range(3)], [[0], [0], [0]]
        s_o, s_on = sem("s_o"), [0]

        def load(src, shape):
            i = rn[0] % NS
            rn[0] += 1
            a, b = shape
            v = ring[:, i, 0:a * b].rearrange("p (a b) -> p a b", a=a)
            m = S_.dma(r_sem[i], r_cnt[i], lambda e: e.dma_start(v, src), *r_free[i])
            return v, m, i

        def mm(o, l, r, start, stop, *marks, skip=False, last=False):
            f = lambda e: e.matmul(o, l, r, start=start, stop=stop, skip_group_check=skip)
            if last:
                return T.do(f, *marks)
            T.plain(f, *marks)

        def tr(o, i, *marks, last=False, k=128):
            f = lambda e: e.transpose(o, i, ident[0:k, 0:k])
            if last:
                return T.do(f, *marks)
            T.plain(f, *marks)

        todo = []

        def pump():
            while todo:
                try:
                    next(todo[0])
                    return
                except StopIteration:
                    todo.pop(0)

        def drain():
            while todo:
                pump()

        def act(o, i, f, *marks, **kw):
            return A.then(lambda e: e.activation(o, i, f, **kw), *marks)

        def tt(o, a, b, op, *marks):
            return V.then(lambda e: e.tensor_tensor(o, a, b, op), *marks)

        def ts(o, a, s1, s2, op0, op1, *marks):
            if s2 is None:
                return V.then(lambda e: e.tensor_scalar(o, a, s1, None, op0), *marks)
            return V.then(lambda e: e.tensor_scalar(o, a, s1, s2, op0, op1), *marks)

        def stt(o, a, s, b, op0, op1, *marks):
            return V.then(lambda e: e.scalar_tensor_tensor(out=o, in0=a, scalar=s, in1=b, op0=op0, op1=op1), *marks)

        def red(o, i, op, *marks):
            return V.then(lambda e: e.tensor_reduce(o, i, AX, op), *marks)

        def vcopy(o, i, *marks):
            return V.then(lambda e: e.tensor_copy(o, i), *marks)

        def recip(o, i, *marks):
            return V.then(lambda e: e.reciprocal(o, i), *marks)

        def rstd(o, ss, n, t1, t2, *marks):
            m = ts(t1, ss, 1.0 / n, EPS, ALU.mult, ALU.add, *marks)
            act(t2, t1, ACT.Ln, m)
            m = act(o, t2, ACT.Exp, scale=-0.5)
            tt(t2, o, o, ALU.mult, m)
            tt(t2, t2, t1, ALU.mult)
            ts(t2, t2, -0.5, 1.5, ALU.mult, ALU.add)
            return tt(o, o, t2, ALU.mult)

        x_d = I["x"].rearrange("a (t p) d -> (a p) t d", p=128)
        A.dma(s_c, s_cn, lambda e: e.dma_start(CW[:, :], I["cw"]))
        stk = S[:, 0:128]
        stk2 = S[:, 128:256]
        r0 = 0
        for nm, nr in ROWS1:
            ap = I[nm]
            src = (ap if len(ap.shape) == 2 else ap.rearrange("(a n) -> a n", a=1)).rearrange("a (k p) -> (a k) p", p=128)
            A.dma(s_c, s_cn, lambda e, r=r0, n=nr, s=src: e.dma_start(stk[r:r + n, :], s))
            r0 += nr
        A.dma(s_c, s_cn, lambda e: e.dma_start(stk2[0:96, :], I["b_mod"].rearrange("a (k p) -> (a k) p", p=128)))
        posr = P[:, 0, 0:256].bitcast(I32)
        posc = P[:, 0, 256:258].bitcast(I32)
        rb = P[:, 0, 300:556]
        A.dma(s_c, s_cn, lambda e: e.dma_start(posr, I["positions"][0, :].partition_broadcast(128)))
        for t in range(2):
            A.dma(s_c, s_cn, lambda e, t=t: e.dma_start(
                posc[:, t:t + 1], I["positions"][0, t * 128:(t + 1) * 128].rearrange("(p a) -> p a", a=1)))
        A.dma(s_c, s_cn, lambda e: e.dma_start(rb, I["rel_bias"].rearrange("b h -> (b h)").partition_broadcast(128)))
        c_in = A.dma(s_c, s_cn, lambda e: e.dma_start(x[:, :, :], x_d))
        pr, i = pair()
        tr(pr[:, 0:102], stk[0:102, :], c_in, k=102)
        m = tr(pr[:, 512:608], stk2[0:96, :], last=True, k=96)
        vcopy(cols[:, :], pr[:, 0:102], m)
        c_col = vcopy(bcol[:, :], pr[:, 512:608])
        tp_free[i] = [c_col]
        off, o = {}, 0
        for nm, nr in ROWS1:
            off[nm] = o
            o += nr

        def col(nm, k=0, n=1):
            return cols[:, off[nm] + k:off[nm] + k + n]

        m = act(cact[:, :], col("c", 0, 16), ACT.Exp, c_col, scale=-1.0)
        ts(cact[:, :], cact[:, :], 1.0, None, ALU.add, None, m)
        recip(cact[:, :], cact[:, :])
        c_act = tt(cact[:, :], cact[:, :], col("c", 0, 16), ALU.mult)

        def tables():
            pf = P[:, 0, 600:602]
            pk = P[:, 0, 640:896]
            ang = P[:, 0, 900:1028]
            kf = P[:, 0, 1100:1228]
            ki = P[:, 0, 1300:1428].bitcast(I32)
            vcopy(pf, posc, c_in)
            vcopy(pk, posr)
            TP = 6.283185307179586
            C1 = 6.28125
            C2 = float(np.float32(TP - C1))
            C2 = float(np.float32(np.round(C2 * 2 ** 21) / 2 ** 21))
            C3 = float(TP - C1 - C2)
            a2 = ang.rearrange("p (t n) -> p t n", t=2)
            for t in range(2):
                ts(a2[:, t, :], CW[:, INV:INV + 64], pf[:, t:t + 1], None, ALU.mult, None)
            for w in (1, 0):
                ts(kf, ang, 1.0 / TP, 0.25 * (1 - w), ALU.mult, ALU.add)
                vcopy(ki, kf)
                vcopy(kf, ki)
                r = cs[:, w, :, :].rearrange("p t n -> p (t n)")
                stt(r, kf, -C1, ang, ALU.mult, ALU.add)
                stt(r, kf, -C2, r, ALU.mult, ALU.add)
                stt(r, kf, -C3, r, ALU.mult, ALU.add)
                if w == 0:
                    ts(r, r, 0.5 * np.pi, None, ALU.add, None)
                m = ts(r, r, 3.1415925, -3.1415925, ALU.min, ALU.max)
                act(r, r, ACT.Sin, m)
            yield
            rel = P[:, 0, 1500:1884]
            hit = P[:, 0, 1900:2284]
            ts(rel[:, 0:128], pk[:, 0:128], -1.0, pf[:, 0:1], ALU.mult, ALU.add)
            ts(rel[:, 128:384], pk, -1.0, pf[:, 1:2], ALU.mult, ALU.add)
            dl = P[:, 0, 2300:2556]
            vcopy(dl[:, 0:8], rb[:, 0:8])
            tt(dl[:, 8:256], rb[:, 8:256], rb[:, 0:248], ALU.subtract)
            cut = [float(j) for j in range(1, 17)] + [float(int(np.ceil(16 * 8 ** (j / 16)))) for j in range(1, 16)]
            for b in range(1, 32):
                ts(hit, rel, cut[b - 1], None, ALU.is_ge, None)
                for h in range(8):
                    for o, n, lo in ((h * 128, 128, 0), (1024 + h * 256, 256, 128)):
                        u = U[:, o:o + n]
                        d = dl[:, b * 8 + h:b * 8 + h + 1]
                        if b == 1:
                            ts(u, hit[:, lo:lo + n], d, dl[:, h:h + 1], ALU.mult, ALU.add)
                        else:
                            stt(u, hit[:, lo:lo + n], d, u, ALU.mult, ALU.add)
                yield

        def modulation(l):
            T.wait(pp_free[0])
            ps = pp[0][:, 0:48]
            for g in range(12):
                for pc in range(4):
                    w, m, i = load(I["w_mod"][l, pc * 512:(pc + 1) * 512, g * 512:(g + 1) * 512]
                                   .rearrange("(k p) n -> p k n", p=128), (4, 512))
                    for b in range(4):
                        for k in range(4):
                            kk = pc * 4 + k
                            fin = mm(ps[:, g * 4 + b:g * 4 + b + 1], w[:, k, b * 128:(b + 1) * 128],
                                     cact[:, kk:kk + 1], g == 0 and pc == 0 and b == 0 and k == 0, kk == 15,
                                     m, c_act, skip=True, last=(b == 3 and k == 3))
                    r_free[i] = [fin]
                    pump()
            pp_free[0] = tt(mcol[:, :], ps, bcol[:, l * 48:(l + 1) * 48], ALU.add, fin, T.now(), A.now())
            ts(mcol[:, 16:32], mcol[:, 16:32], 1.0, None, ALU.add, None)
            return tt(mcol[:, 16:32], mcol[:, 16:32], col("norm_gain", 16 * l, 16), ALU.mult)

        ss = sm[:, 0:24]
        q1, q2, q3 = sm[:, 24:48], sm[:, 48:72], sm[:, 72:96]
        mx = sm[:, 96:104]
        rs = sm[:, 104:112]
        m8 = sm[:, 112:120]

        def row_norm(meta):
            A.wait(V.now(), T.now())
            for t in range(2):
                act(P[:, t, 0:D], x[:, t, :], ACT.Square, accum_out=ss[:, t:t + 1])
            if meta:
                act(P[0:16, 1, D:2 * D], P[0:16, 0, D:2 * D], ACT.Square, s_meta, accum_out=ss[0:16, 2:3])
                rstd(q1[0:16, 2:3], ss[0:16, 2:3], D, q2[0:16, 2:3], q3[0:16, 2:3], A.now())
            m = rstd(q1[:, 0:2], ss[:, 0:2], D, q2[:, 0:2], q3[:, 0:2], A.now())
            for t in range(2):
                m2 = act(P[:, t, 0:D], x[:, t, :], ACT.Copy, m, scale=q1[:, t:t + 1])
            if meta:
                m2 = act(P[0:16, 1, D:2 * D], P[0:16, 0, D:2 * D], ACT.Copy, scale=q1[0:16, 2:3])
            return m2

        def to_hT(src, ready, ev, extra=()):
            for k0 in range(0, NK, 4):
                pr, i = pair()
                for k in range(k0, k0 + 4):
                    for t in range(2):
                        o = (k - k0) * 256 + t * 128
                        m = tr(pr[:, o:o + 128], src(t, k), ready, last=(k == k0 + 3 and t == 1))
                fr = []
                for k in range(k0, k0 + 4):
                    fr.append(ev(k, hT[:, k, 0:256], pr[:, (k - k0) * 256:(k - k0 + 1) * 256], m))
                tp_free[i] = fr
            return fr

        def project(wd, groups, ready, store, after=None, meta=None, pumping=True):
            for n, (c0, w) in enumerate(groups):
                bk = [(n % 2) * 2, (n % 2) * 2 + 1]
                md = meta(c0, w) if meta else None
                if md:
                    pm, mi = pair()
                for pc in range(4):
                    wt, m, i = load(wd[pc * 512:(pc + 1) * 512, c0:c0 + w]
                                    .rearrange("(k p) n -> p k n", p=128), (4, w))
                    for t in range(2):
                        for k in range(4):
                            kk = pc * 4 + k
                            fin = mm(pp[bk[t]][:, 0:w], hT[:, kk, t * 128:(t + 1) * 128], wt[:, k, :],
                                     kk == 0, kk == 15, m, *ready, pp_free[bk[t]] if kk == 0 else None,
                                     last=(k == 3))
                        if pc == 3:
                            pp_free[bk[t]] = store(n, c0, w, t, pp[bk[t]][:, 0:w], fin)
                    if md:
                        lo, dst = md
                        for k in range(4):
                            kk = pc * 4 + k
                            fin = mm(pm[0:16, 0:w - lo], hT[:, kk, 256:272], wt[:, k, lo:w],
                                     kk == 0, kk == 15, last=(k == 3))
                        if pc == 3:
                            tp_free[mi] = [act(dst, pm[0:16, 0:w - lo], ACT.Copy, fin)]
                    r_free[i] = [fin]
                    if pumping and not md:
                        pump()
                if after:
                    after(n)

        def head_rms(v, nh, p, *marks):
            f = v.rearrange("p (h d) -> p h d", h=nh)
            sq = S[0:p, 0:nh * 128].rearrange("p (h d) -> p h d", h=nh)
            tt(sq, f, f, ALU.mult, *marks)
            red(ss[0:p, 0:nh], sq, ALU.add)
            rstd(q1[0:p, 0:nh], ss[0:p, 0:nh], 128, q2[0:p, 0:nh], q3[0:p, 0:nh])
            return tt(f, f, q1[0:p, 0:nh].unsqueeze(2).to_broadcast([p, nh, 128]), ALU.mult)

        def gate(t, g0, y0, silu):
            g = P[:, t, g0:g0 + 1024]
            y = P[:, t, y0:y0 + 1024]
            e = S[:, 0:1024]
            m = act(e, g, ACT.Exp, V.now(), T.now(), scale=-1.0)
            ts(e, e, 1.0, None, ALU.add, None, m)
            recip(e, e)
            if silu:
                tt(e, e, g, ALU.mult)
            return tt(y, y, e, ALU.mult)

        def turn_heads(src, dst, nh, ready, **kw):
            for h0 in range(0, nh, 4):
                n = min(4, nh - h0)
                pr, i = pair()
                for h in range(n):
                    for t in range(2):
                        o = h * 256 + t * 128
                        m = tr(pr[:, o:o + 128], src(t, h0 + h), ready, last=(h == n - 1 and t == 1))
                r = act(dst[:, h0:h0 + n, :], pr[:, 0:n * 256].rearrange("p (h n) -> p h n", h=n), ACT.Copy,
                        m, V.now(), **kw)
                tp_free[i] = [r]
                yield r

        def sparse(l):
            V.then(lambda e: e.memset(S[:, 0:512], 0.0), A.now(), T.now())
            for t in range(2):
                ki = P[:, t, KI:KI + 64]
                vcopy(S[:, t * 256:t * 256 + 64], ki, A.now())
                m = vcopy(S[:, t * 256 + 192:t * 256 + 256], ki)
            pr, i = pair()
            for e_ in range(2):
                for t in range(2):
                    o = e_ * 256 + t * 128
                    mt = tr(pr[:, o:o + 128], S[:, t * 256 + e_ * 128:t * 256 + e_ * 128 + 128], m,
                            last=(e_ == 1 and t == 1))
            tp_free[i] = [vcopy(KIT[:, :, :].rearrange("p a n -> p (a n)"), pr[:, 0:512], mt)]
            yield
            for mq in turn_heads(lambda t, h: P[:, t, QI + h * 128:QI + (h + 1) * 128], TA, 8, V.now()):
                yield
            yield
            for t in range(2):
                nk = 128 * (t + 1)
                used = [V.now(), V.now()]
                for g in range(4):
                    pr, i = pair()
                    for b in range(2):
                        for e_ in range(2):
                            m = mm(pr[:, b * 512 + e_ * nk:b * 512 + (e_ + 1) * nk],
                                   TA[:, 2 * g + b, t * 128:(t + 1) * 128], KIT[:, e_, 0:nk], True, True,
                                   mq, V.now(), last=(b == 1 and e_ == 1))
                    r = S[:, 512 + (g % 2) * 1024:512 + (g % 2) * 1024 + 4 * nk]
                    mr = act(r.rearrange("p (b n) -> p b n", b=2),
                             pr.rearrange("p (b n) -> p b n", b=2)[:, :, 0:2 * nk], ACT.Relu, m, used[g % 2])
                    tp_free[i] = [mr]
                    for h in range(4):
                        wh = P[:, t, WI + 4 * g + h:WI + 4 * g + h + 1]
                        rh = r[:, h * nk:(h + 1) * nk]
                        if g == 0 and h == 0:
                            ts(IW[:, 0:nk], rh, wh, None, ALU.mult, None, mr)
                        else:
                            used[g % 2] = stt(IW[:, 0:nk], rh, wh, IW[:, 0:nk], ALU.mult, ALU.add, mr)
                    yield
                w = IW[:, 0:nk]
                tt(w[:, nk - 128:nk], w[:, nk - 128:nk], CW[:, NTT:NTT + 128], ALU.add)
                for _ in range(8):
                    V.then(lambda e, w=w: e.max(m8, w))
                    V.then(lambda e, w=w: e.match_replace(w, m8, w, TAKEN))
                ng = NEG[:, t * 128:t * 128 + nk]
                ts(ng, w, -2.0e38, NEGV, ALU.is_gt, ALU.mult)
                tt(ng[:, nk - 128:nk], ng[:, nk - 128:nk], CW[:, NTT:NTT + 128], ALU.add)
                yield
            for t in range(2):
                head_rms(P[:, t, QA:QA + 1024], 8, 128, A.now())
                mk = head_rms(P[:, t, KA:KA + 128], 1, 128)
                yield
            gk = cols[:, off["k_norm_gain"] + l:off["k_norm_gain"] + l + 1]
            gq = cols[:, off["q_norm_gain"] + l:off["q_norm_gain"] + l + 1]
            for _ in turn_heads(lambda t, h: P[:, t, KA:KA + 128],
                                KAT[:, :].rearrange("p (a n) -> p a n", a=1), 1, mk, scale=gk):
                pass
            for mq in turn_heads(lambda t, h: P[:, t, QA + h * 128:QA + (h + 1) * 128], TA, 8, mk, scale=gq):
                yield
            yield
            for t in range(2):
                nk = 128 * (t + 1)
                for g in range(2):
                    pr, i = pair()
                    for h in range(4):
                        o = (h // 2) * 512 + (h % 2) * nk
                        m = mm(pr[:, o:o + nk], TA[:, 4 * g + h, t * 128:(t + 1) * 128], KAT[:, 0:nk], True, True,
                               mq, last=(h == 3))
                    bo = (0 if t == 0 else 1024) + 4 * g * nk
                    s0 = S[:, 0:4 * nk]
                    tp_free[i] = [stt(s0.rearrange("p (b n) -> p b n", b=2),
                                      pr.rearrange("p (b n) -> p b n", b=2)[:, :, 0:2 * nk], SC,
                                      U[:, bo:bo + 4 * nk].rearrange("p (b n) -> p b n", b=2),
                                      ALU.mult, ALU.add, m, T.now(), A.now())]
                    s4 = s0.rearrange("p (h n) -> p h n", h=4)
                    ng = NEG[:, t * 128:t * 128 + nk]
                    tt(s4, s4, ng.unsqueeze(1).to_broadcast([128, 4, nk]), ALU.add)
                    red(mx[:, 0:4], s4, ALU.max)
                    m = ts(mx[:, 0:4], mx[:, 0:4], -1.0, None, ALU.mult, None)
                    for h in range(4):
                        me = A.do(lambda e, h=h, s4=s4: e.activation(
                            s4[:, h, :], s4[:, h, :], ACT.Exp, bias=mx[:, h:h + 1], accum_out=rs[:, h:h + 1]), m)
                    yield
                    pr, i = pair()
                    nt = t + 1
                    for h in range(4):
                        for kt in range(nt):
                            o = (h * nt + kt) * 128
                            m = tr(pr[:, o:o + 128], s4[:, h, kt * 128:(kt + 1) * 128], me,
                                   last=(h == 3 and kt == nt - 1))
                    pT = S[:, 1024:1024 + 512 * nt]
                    mp = vcopy(pT, pr[:, 0:512 * nt], m)
                    tp_free[i] = [mp]
                    recip(rs[:, 0:4], rs[:, 0:4], me)
                    yield
                    pr, i = pair()
                    for h in range(4):
                        for kt in range(nt):
                            o = (h * nt + kt) * 128
                            m = mm(pr[:, h * 128:(h + 1) * 128], pT[:, o:o + 128], P[:, kt, VA:VA + 128],
                                   kt == 0, kt == nt - 1, mp, A.now(), last=(h == 3 and kt == nt - 1))
                    tp_free[i] = [tt(P[:, t, QA + 512 * g:QA + 512 * (g + 1)].rearrange("p (h d) -> p h d", h=4),
                                     pr[:, 0:512].rearrange("p (h d) -> p h d", h=4),
                                     rs[:, 0:4].unsqueeze(2).to_broadcast([128, 4, 128]), ALU.mult, m)]
                    yield
            for t in range(2):
                gate(t, GA, QA, True)
                yield

        dm_free = [None, None]

        def retention():
            for c0 in (QB, KB):
                for t in range(2):
                    v = P[:, t, c0:c0 + 1024].rearrange("p (h d) -> p h d", h=8)
                    x1, x2 = v[:, :, 0:64], v[:, :, 64:128]
                    co = cs[:, 0, t, :].unsqueeze(1).to_broadcast([128, 8, 64])
                    si = cs[:, 1, t, :].unsqueeze(1).to_broadcast([128, 8, 64])
                    t1, t2, t3 = (S[:, j * 512:(j + 1) * 512].rearrange("p (h d) -> p h d", h=8) for j in range(3))
                    tt(t1, x1, co, ALU.mult, A.now(), T.now())
                    tt(t2, x2, si, ALU.mult)
                    tt(t3, x1, si, ALU.mult)
                    tt(x2, x2, co, ALU.mult)
                    tt(x1, t1, t2, ALU.subtract)
                    mr = tt(x2, x2, t3, ALU.add)
                    yield
            for _ in turn_heads(lambda t, h: P[:, t, QB + h * 128:QB + (h + 1) * 128], TA, 8, mr):
                yield
            for mq in turn_heads(lambda t, h: P[:, t, KB + h * 128:KB + (h + 1) * 128], TB[:, :, 0:256], 8, mr, scale=SC):
                yield
            for g in range(4):
                b = g % 2
                dmt = U[:, 3072 + b * 768:3072 + (b + 1) * 768]
                md = G.dma(s_d[b], s_dn[b], lambda e, g=g, dmt=dmt: e.dma_start(
                    dmt, I["dm"][:, 2 * g:2 * g + 2, :].rearrange("p h n -> p (h n)")), dm_free[b])
                pr, i = pair()
                for h in range(2):
                    hh = 2 * g + h
                    mm(pr[:, h * 512:h * 512 + 256], TB[:, hh, 0:128], TA[:, hh, :], True, True, mq)
                    m = mm(pr[:, h * 512 + 256:h * 512 + 384], TB[:, hh, 128:256], TA[:, hh, 128:256], True, True,
                           last=True)
                st = S[:, b * 768:(b + 1) * 768].rearrange("p (h n) -> p h n", h=2)
                ms = tt(st, pr.rearrange("p (h n) -> p h n", h=2)[:, :, 0:384],
                        dmt.rearrange("p (h n) -> p h n", h=2), ALU.mult, m, md, T.now())
                tp_free[i] = [ms]
                dm_free[b] = ms
                yield
                pr, i = pair()
                for h in range(2):
                    vb = VB + (2 * g + h) * 128
                    mm(pr[:, h * 128:(h + 1) * 128], st[:, h, 0:128], P[:, 0, vb:vb + 128], True, True, ms, A.now())
                    mm(pr[:, 512 + h * 128:640 + h * 128], st[:, h, 128:256], P[:, 0, vb:vb + 128], True, False)
                    m = mm(pr[:, 512 + h * 128:640 + h * 128], st[:, h, 256:384], P[:, 1, vb:vb + 128], False, True,
                           last=True)
                vcopy(P[:, 0, QB + g * 256:QB + (g + 1) * 256], pr[:, 0:256], m)
                mo = vcopy(P[:, 1, QB + g * 256:QB + (g + 1) * 256], pr[:, 512:768])
                tp_free[i] = [mo]
                yield
            for t in range(2):
                v = P[:, t, QB:QB + 1024].rearrange("p (h d) -> p h d", h=8)
                red(ss[:, 0:8], v, ALU.add)
                ts(ss[:, 0:8], ss[:, 0:8], -1.0 / 128, None, ALU.mult, None)
                tt(v, v, ss[:, 0:8].unsqueeze(2).to_broadcast([128, 8, 128]), ALU.add)
                head_rms(P[:, t, QB:QB + 1024], 8, 128, T.now(), A.now())
                gate(t, GB, QB, True)
                yield

        def cgroups(*spans):
            r = []
            for c0, n, w in spans:
                r += [(c0 + j * w, w) for j in range(n)]
            return r

        def store_p(n, c0, w, t, ps, m):
            return act(P[:, t, c0:c0 + w], ps, ACT.Copy, m)

        todo.append(tables())
        for l in range(2):
            m = modulation(l)
            drain()
            mn = row_norm(False)
            ev = lambda k, o, ps, mk: ts(o, ps, mcol[:, 16 + k:17 + k], mcol[:, k:k + 1], ALU.mult, ALU.add, mk)
            to_hT(lambda t, k: P[:, t, k * 128:(k + 1) * 128], mn, ev)
            A.wait(T.now())
            groups = cgroups((QI, 3, 368), (KA, 1, 256), (QA, 2, 512), (GA, 2, 512), (QB, 8, 512))

            def after(n):
                if n == 7:
                    todo.append(sparse(l))
                if n == 15:
                    todo.append(retention())

            project(I["w_in"][l], groups, [V.now()], store_p, after)
            drain()
            gr = off["ret_norm_gain"] + 8 * l

            def ev(k, o, ps, mk):
                if k < 8:
                    return act(o, ps, ACT.Copy, mk)
                return act(o, ps, ACT.Copy, mk, scale=cols[:, gr + k - 8:gr + k - 7])

            my = V.now()
            ysrc = lambda t, k: P[:, t, (QA if k < 8 else QB - 1024) + k * 128:(QA if k < 8 else QB - 1024) + (k + 1) * 128]
            gb = TAB[:, 0:2048]
            for k0 in range(0, NK, 8):
                for k in range(k0, k0 + 8):
                    md = ts(S[:, (k - k0) * 128:(k - k0 + 1) * 128], ident, mcol[:, 32 + k:33 + k], None, ALU.mult,
                            None, T.now(), A.now())
                pr, i = pair()
                for b in range(2):
                    m = mm(pr[:, b * 512:(b + 1) * 512], ones, S[:, b * 512:(b + 1) * 512], True, True, md, last=True)
                tp_free[i] = [vcopy(gb[:, k0 * 128:(k0 + 8) * 128], pr[:, :], m)]
            to_hT(ysrc, my, ev)
            ready = A.now()

            def store_x(n, c0, w, t, ps, m):
                tmp = S[:, 1024 + t * 512:1024 + (t + 1) * 512]
                r = tt(tmp, ps, gb[:, c0:c0 + w], ALU.mult, m)
                tt(x[:, t, c0:c0 + w], x[:, t, c0:c0 + w], tmp, ALU.add)
                return r

            project(I["w_out"][l], cgroups((0, 4, 512)), [ready], store_x, pumping=False)

        PM = U[0:16, 0:4104]
        s_meta = G.dma(s_m[0], s_mn[0], lambda e: e.dma_start(P[0:16, 0, D:2 * D], I["meta_tokens_2"]), V.now(), T.now(), A.now())
        mn = row_norm(True)
        ev = lambda k, o, ps, mk: ts(o, ps, col("norm_mix_2", k), None, ALU.mult, None, mk)
        to_hT(lambda t, k: P[:, t, k * 128:(k + 1) * 128], mn, ev)
        pr, i = pair()
        for k in range(NK):
            m = tr(pr[:, k * 16:(k + 1) * 16], P[0:16, 1, D + k * 128:D + (k + 1) * 128], k=16, last=(k == 15))
        tp_free[i] = [tt(hT[:, :, 256:272], pr[:, 0:256].rearrange("p (k n) -> p k n", k=16),
                         col("norm_mix_2", 0, 16).unsqueeze(2).to_broadcast([128, 16, 16]), ALU.mult, m)]
        bf = S[:, 2552:2560]
        m_bf = G.dma(s_m[1], s_mn[1], lambda e: e.dma_start(bf, I["b_forget_2"].rearrange("a h -> (a h)").partition_broadcast(128)))
        A.wait(T.now(), V.now())

        def meta(c0, w):
            for a, b in ((SK, MSK), (SV, MSV), (FK, MFK), (FV, MFV)):
                if a <= c0 < a + 1024:
                    return 0, PM[:, b + c0 - a:b + c0 - a + w]
            if c0 + w > FL:
                return FL - c0, PM[:, MFL:MFL + 8]
            return None

        def turn_keys(src, msrc, ready, **kw):
            for mk in turn_heads(src, TB[:, :, 16:272], 8, ready, **kw):
                yield mk
            pr, i = pair()
            for h in range(8):
                m = tr(pr[:, h * 16:(h + 1) * 16], msrc(h), k=16, last=(h == 7))
            mk = act(TB[:, :, 0:16], pr[:, 0:128].rearrange("p (h n) -> p h n", h=8), ACT.Copy, m, **kw)
            tp_free[i] = [mk]
            yield mk

        def stick():
            for _ in turn_heads(lambda t, h: P[:, t, SQ + h * 128:SQ + (h + 1) * 128], TA, 8, A.now()):
                yield
            for mk in turn_keys(lambda t, h: P[:, t, SK + h * 128:SK + (h + 1) * 128],
                                lambda h: PM[:, MSK + h * 128:MSK + (h + 1) * 128], A.now()):
                yield
            z = S[:, 0:1280].rearrange("p (h n) -> p h n", h=2)
            L = S[:, 1280:2560].rearrange("p (h n) -> p h n", h=2)
            zx, zm = z[:, :, 0:384], z[0:16, :, 384:640]
            Lx, Lm = L[:, :, 0:384], L[0:16, :, 384:640]
            parts = ((zx, Lx), (zm, Lm))
            for g in range(4):
                pr, i = pair()
                for h in range(2):
                    hh = 2 * g + h
                    mm(pr[:, h * 512:h * 512 + 256], TB[:, hh, 16:144], TA[:, hh, :], True, True, mk)
                    m = mm(pr[:, h * 512 + 256:h * 512 + 384], TB[:, hh, 144:272], TA[:, hh, 128:256], True, True,
                           last=True)
                tp_free[i] = [ts(zx, pr.rearrange("p (h n) -> p h n", h=2)[:, :, 0:384], SC, None, ALU.mult, None,
                                 m, T.now(), A.now(), m_bf)]
                pr, i = pair()
                for h in range(2):
                    m = mm(pr[0:16, h * 256:(h + 1) * 256], TB[:, 2 * g + h, 0:16], TA[:, 2 * g + h, :], True, True,
                           last=True)
                tp_free[i] = [ts(zm, pr[0:16, 0:512].rearrange("p (h n) -> p h n", h=2), SC, None, ALU.mult, None, m)]
                for a, b in parts:
                    act(b, a, ACT.Abs, V.now())
                    act(b, b, ACT.Exp, scale=-1.0)
                    m = act(b, b, ACT.Ln, bias=1.0)
                    stt(b, a, 0.0, b, ALU.max, ALU.add, m)
                for c in (0, 256):
                    tt(Lx[:, :, c:c + 128], Lx[:, :, c:c + 128],
                       CW[:, SM:SM + 128].unsqueeze(1).to_broadcast([128, 2, 128]), ALU.mult)
                    tt(zx[:, :, c:c + 128], zx[:, :, c:c + 128],
                       CW[:, NSM:NSM + 128].unsqueeze(1).to_broadcast([128, 2, 128]), ALU.add)
                mL = V.now()
                yield
                pr, i = pair()
                trl = CW[:, TRL:TRL + 128]
                for h in range(2):
                    o = h * 512
                    mm(pr[:, o:o + 256], trl, L[:, h, 0:256], True, False, mL)
                    mm(pr[:, o + 128:o + 256], ones, L[:, h, 256:384], False, True)
                    m = mm(pr[:, o + 256:o + 384], trl, L[:, h, 256:384], True, True, last=True)
                tp_free[i] = [tt(zx, zx, pr.rearrange("p (h n) -> p h n", h=2)[:, :, 0:384], ALU.subtract, m)]
                act(zx, zx, ACT.Exp, V.now())
                pr, i = pair()
                for h in range(2):
                    o = h * 256
                    mm(pr[0:16, o:o + 256], trl[0:16, 0:16], L[0:16, h, 384:640], True, False)
                    mm(pr[0:16, o:o + 256], ones[:, 0:16], L[:, h, 0:256], False, False)
                    m = mm(pr[0:16, o + 128:o + 256], ones[:, 0:16], L[:, h, 256:384], False, True, last=True)
                tp_free[i] = [tt(zm, zm, pr[0:16, 0:512].rearrange("p (h n) -> p h n", h=2), ALU.subtract, m)]
                mw = act(zm, zm, ACT.Exp, V.now())
                yield
                pr, i = pair()
                for h in range(2):
                    vc = SV + (2 * g + h) * 128
                    vm = PM[:, MSV + (2 * g + h) * 128:MSV + (2 * g + h + 1) * 128]
                    o = h * 128
                    mm(pr[:, o:o + 128], z[:, h, 0:128], P[:, 0, vc:vc + 128], True, False, mw)
                    mm(pr[:, o:o + 128], z[0:16, h, 384:512], vm, False, True)
                    o += 512
                    mm(pr[:, o:o + 128], z[:, h, 128:256], P[:, 0, vc:vc + 128], True, False)
                    mm(pr[:, o:o + 128], z[:, h, 256:384], P[:, 1, vc:vc + 128], False, False)
                    m = mm(pr[:, o:o + 128], z[0:16, h, 512:640], vm, False, True, last=True)
                for t in range(2):
                    mo = vcopy(P[:, t, SQ + g * 256:SQ + (g + 1) * 256], pr[:, t * 512:t * 512 + 256], m)
                tp_free[i] = [mo]
                yield
            yield from out_rms(SQ)

        def out_rms(c0):
            for t in range(2):
                v = P[:, t, c0:c0 + 1024]
                tt(S[:, 0:1024], v, v, ALU.mult, A.now(), T.now())
                red(ss[:, 0:1], S[:, 0:1024], ALU.add)
                rstd(q1[:, 0:1], ss[:, 0:1], 1024, q2[:, 0:1], q3[:, 0:1])
                ts(v, v, q1[:, 0:1], None, ALU.mult, None)
                yield

        def fox():
            for t in range(3):
                p = 16 if t == 2 else 128
                v = PM[:, MFL:MFL + 8] if t == 2 else P[:, t, FL:FL + 8]
                f, e1 = lf[0:p, t, :], q1[0:p, 0:8]
                tt(f, v, bf_s[0:p, :], ALU.add, A.now())
                act(e1, f, ACT.Abs, V.now())
                act(e1, e1, ACT.Exp, scale=-1.0)
                m = act(e1, e1, ACT.Ln, bias=1.0)
                stt(f, f, 0.0, e1, ALU.min, ALU.subtract, m)
            mf = V.now()
            pr, i = pair()
            tru = CW[:, TRU:TRU + 128]
            mm(pr[:, 0:8], ones[0:16, :], lf[0:16, 2, :], True, False, mf)
            mm(pr[:, 0:8], tru, lf[:, 0, :], False, True)
            mm(pr[:, 8:16], ones[0:16, :], lf[0:16, 2, :], True, False)
            mm(pr[:, 8:16], ones, lf[:, 0, :], False, False)
            m = mm(pr[:, 8:16], tru, lf[:, 1, :], False, True, last=True)
            tp_free[i] = [vcopy(fcol[:, :, :].rearrange("p t h -> p (t h)"), pr[:, 0:16], m)]
            for t in range(2):
                ts(lf[:, t, :], lf[:, t, :], -1.0 / SC, None, ALU.mult, None)
            mf = ts(lf[0:16, 2, :], lf[0:16, 2, :], -1.0 / SC, None, ALU.mult, None)
            yield
            for c0 in (FQ, FK):
                for t in range(2):
                    head_rms(P[:, t, c0:c0 + 1024], 8, 128, A.now(), T.now())
                    yield
            mr = head_rms(PM[:, MFK:MFK + 1024], 8, 16)
            yield
            gq, gk = col("fox_q_gain_2"), col("fox_k_gain_2")
            for _ in turn_heads(lambda t, h: P[:, t, FQ + h * 128:FQ + (h + 1) * 128], TA, 8, mr, scale=gq):
                yield
            for mk in turn_keys(lambda t, h: P[:, t, FK + h * 128:FK + (h + 1) * 128],
                                lambda h: PM[:, MFK + h * 128:MFK + (h + 1) * 128], mr, scale=gk):
                yield
            for g in range(4):
                lb = S[:, 1792:2560].rearrange("p (h t n) -> p h t n", h=2, t=3)
                for h in range(2):
                    for t in range(3):
                        p = 16 if t == 2 else 128
                        mb = ts(lb[0:p, h, t, :], ones[0:p, :], lf[0:p, t, 2 * g + h:2 * g + h + 1], None, ALU.mult,
                                None, T.now())
                for t in range(2):
                    nk = 144 + 128 * t
                    pr, i = pair()
                    for h in range(2):
                        o = h * 512
                        mm(pr[:, o:o + nk], TA[:, 2 * g + h, t * 128:(t + 1) * 128], TB[:, 2 * g + h, 0:nk], True, False,
                           mk, mb)
                        mm(pr[:, o:o + 16], lb[0:16, h, 2, :], tru[0:16, 0:16], False, False)
                        for c in range(16, nk, 128):
                            mm(pr[:, o + c:o + c + 128], lb[0:16, h, 2, :], ones[0:16, :], False, False)
                        m = mm(pr[:, o + 16:o + 144], lb[:, h, 0, :], tru, False, t == 0, last=True)
                        if t == 1:
                            mm(pr[:, o + 144:o + 272], lb[:, h, 0, :], ones, False, False)
                            m = mm(pr[:, o + 144:o + 272], lb[:, h, 1, :], tru, False, True, last=True)
                    s = S[:, 0:2 * nk].rearrange("p (h n) -> p h n", h=2)
                    tp_free[i] = [ts(s, pr.rearrange("p (h n) -> p h n", h=2)[:, :, 0:nk], SC, None, ALU.mult, None,
                                     m, A.now())]
                    dg = s[:, :, nk - 128:nk]
                    tt(dg, dg, CW[:, NTT:NTT + 128].unsqueeze(1).to_broadcast([128, 2, 128]), ALU.add)
                    red(mx[:, 0:2], s, ALU.max)
                    fc = fcol[:, t, 2 * g:2 * g + 2]
                    tt(mx[:, 0:2], mx[:, 0:2], fc, ALU.add)
                    m = tt(mx[:, 0:2], fc, mx[:, 0:2], ALU.subtract)
                    for h in range(2):
                        me = A.do(lambda e, h=h, s=s: e.activation(
                            s[:, h, :], s[:, h, :], ACT.Exp, bias=mx[:, h:h + 1], accum_out=rs[:, h:h + 1]), m)
                    yield
                    pr, i = pair()
                    nt = t + 2
                    for h in range(2):
                        tr(pr[0:16, h * 512:h * 512 + 128], s[:, h, 0:16], me)
                        for kt in range(1, nt):
                            m = tr(pr[:, h * 512 + kt * 128:h * 512 + (kt + 1) * 128],
                                   s[:, h, 16 + (kt - 1) * 128:16 + kt * 128], last=True)
                    pT = S[:, 1024:1792].rearrange("p (h n) -> p h n", h=2)
                    prh = pr.rearrange("p (h n) -> p h n", h=2)
                    vcopy(pT[0:16, :, 0:128], prh[0:16, :, 0:128], m)
                    mp = vcopy(pT[:, :, 128:nt * 128], prh[:, :, 128:nt * 128])
                    tp_free[i] = [mp]
                    recip(rs[:, 0:2], rs[:, 0:2], me)
                    yield
                    pr, i = pair()
                    for h in range(2):
                        o = h * 128
                        hv = (2 * g + h) * 128
                        mm(pr[:, o:o + 128], pT[0:16, h, 0:128], PM[:, MFV + hv:MFV + hv + 128], True, False, mp)
                        for kt in range(1, nt):
                            m = mm(pr[:, o:o + 128], pT[:, h, kt * 128:(kt + 1) * 128],
                                   P[:, kt - 1, FV + hv:FV + hv + 128], False, kt == nt - 1, last=True)
                    tp_free[i] = [tt(P[:, t, FQ + g * 256:FQ + (g + 1) * 256].rearrange("p (h d) -> p h d", h=2),
                                     pr[:, 0:256].rearrange("p (h d) -> p h d", h=2),
                                     rs[:, 0:2].unsqueeze(2).to_broadcast([128, 2, 128]), ALU.mult, m)]
                    yield
            yield from out_rms(FQ)
            for t in range(2):
                gate(t, FG, FQ, False)
                yield

        bf_s = sm[:, 120:128]
        vcopy(bf_s, bf, m_bf)
        groups = cgroups((SQ, 6, 512), (FQ, 6, 512), (FG, 3, 344))

        def after(n):
            if n == 5:
                todo.append(stick())
            if n == 14:
                todo.append(fox())

        project(I["w_in_2"][0], groups, [V.now()], store_p, after, meta)
        drain()
        ysrc = lambda t, k: P[:, t, (SQ if k < 8 else FQ - 1024) + k * 128:(SQ if k < 8 else FQ - 1024) + (k + 1) * 128]
        g0 = off["sb_out_gain_2"]
        ev = lambda k, o, ps, mk: act(o, ps, ACT.Copy, mk, scale=cols[:, g0 + k:g0 + k + 1])
        to_hT(ysrc, V.now(), ev)

        def store_h(n, c0, w, t, ps, m):
            return tt(x[:, t, c0:c0 + w], x[:, t, c0:c0 + w], ps, ALU.add, m)

        project(I["w_out_2"][0], cgroups((0, 4, 512)), [A.now()], store_h, pumping=False)

        nf = U[:, 0:2048]
        m_nf = G.dma(s_m[2], s_mn[2], lambda e: e.dma_start(nf, I["norm_ffn_2"][0, :].partition_broadcast(128)),
                     T.now(), A.now(), V.now())
        mn = row_norm(False)
        hn = P[:, 0, 0:2048], P[:, 0, 2048:4096]
        for t in (1, 0):
            mh = tt(hn[t], P[:, t, 0:D], nf, ALU.mult, mn, m_nf)
        ev = lambda k, o, ps, mk: act(o, ps, ACT.Copy, mk)
        to_hT(lambda t, k: hn[t][:, k * 128:(k + 1) * 128], mh, ev)
        ready = A.now()
        qT = TAB[:, 0:4096].rearrange("p (b n) -> p b n", b=16)
        for g in range(4):
            bk = [(g % 2) * 2, (g % 2) * 2 + 1]
            for pc in range(4):
                wt, m, i = load(I["peer_w_query_2"][0, pc * 512:(pc + 1) * 512, g * 512:(g + 1) * 512]
                                .rearrange("(k p) n -> p k n", p=128), (4, 512))
                for b in range(4):
                    ps = pp[bk[b // 2]][:, (b % 2) * 256:(b % 2 + 1) * 256]
                    for k in range(4):
                        kk = pc * 4 + k
                        fin = mm(ps, wt[:, k, b * 128:(b + 1) * 128], hT[:, kk, 0:256],
                                 kk == 0 and b % 2 == 0, kk == 15, m, ready,
                                 pp_free[bk[b // 2]] if kk == 0 else None, skip=True, last=(k == 3))
                r_free[i] = [fin]
            for b in range(2):
                pp_free[bk[b]] = act(qT[:, 4 * g + 2 * b:4 * g + 2 * b + 2, :],
                                     pp[bk[b]][:, :].rearrange("p (b n) -> p b n", b=2), ACT.Copy, fin)
        sk, m, i = load(I["peer_sub_keys_2"][0].rearrange("h s n c -> n (h s) c"), (16, 128))
        skT = S[:, 0:2048]
        for b0 in (0, 8):
            pr, pi = pair()
            for b in range(8):
                mt = tr(pr[:, b * 128:(b + 1) * 128], sk[:, b0 + b, :], m, last=True)
            tp_free[pi] = [vcopy(skT[:, b0 * 128:(b0 + 8) * 128], pr[:, :], mt)]
        r_free[i] = [mt]
        msk = V.now()

        hx = hT[:, :, :].rearrange("p k n -> p (k n)")
        oh = hx[:, 0:2048].rearrange("p (h k a) -> p h k a", h=8, k=16)
        tv = hx[:, 2048:2304].rearrange("p (b k) -> p b k", b=16)
        ti = hx[:, 2304:2560].bitcast(U32).rearrange("p (b k) -> p b k", b=16)
        tf = hx[:, 2560:2816].rearrange("p (b k) -> p b k", b=16)
        bv = hx[:, 2816:2944].rearrange("p (h k) -> p h k", h=8)
        bj = hx[:, 2944:3072].bitcast(U32)
        bh = hx[:, 3072:3200].bitcast(U32)
        fa = hx[:, 3200:3328]
        fi = [hx[:, 3328:3456], hx[:, 3456:3584]]
        aa = hx[:, 3584:3840].rearrange("p (t j) -> p t j", t=2)
        co = hx[:, 3840:4096].rearrange("p (t j) -> p t j", t=2)
        ix = hx[:, 4096:4352].bitcast(U32).rearrange("p (t j) -> p t j", t=2)
        sc = U[:, 0:2048]
        ca = U[:, 2048:4096]
        V.wait(T.now(), A.now())

        def choose(t):
            for b0 in (0, 8):
                pr, i = pair()
                for b in range(8):
                    m = mm(pr[:, b * 128:(b + 1) * 128], qT[:, b0 + b, t * 128:(t + 1) * 128],
                           skT[:, (b0 + b) * 128:(b0 + b + 1) * 128], True, True, msk, A.now(), last=(b == 7))
                tp_free[i] = [act(sc[:, b0 * 128:(b0 + 8) * 128], pr[:, :], ACT.Copy, m, V.now())]

            def top16(src, val, idx):
                V.then(lambda e: e.max(val[:, 0:8], src), A.now())
                V.then(lambda e: e.max_index(idx[:, 0:8], val[:, 0:8], src))
                V.then(lambda e: e.match_replace(src, val[:, 0:8], src, TAKEN))
                V.then(lambda e: e.max(val[:, 8:16], src))
                V.then(lambda e: e.max_index(idx[:, 8:16], val[:, 8:16], src))

            for b in range(16):
                top16(sc[:, b * 128:(b + 1) * 128], tv[:, b, :], ti[:, b, :])
            vcopy(tf, ti)
            t0 = tv.rearrange("p (h s) k -> p h s k", s=2)
            f0 = tf.rearrange("p (h s) k -> p h s k", s=2)
            c4 = ca.rearrange("p (h a b) -> p h a b", h=8, a=16)
            tt(c4, t0[:, :, 0, :].unsqueeze(3).to_broadcast([128, 8, 16, 16]),
               t0[:, :, 1, :].unsqueeze(2).to_broadcast([128, 8, 16, 16]), ALU.add)
            bj8 = bj.rearrange("p (h k) -> p h k", h=8)
            for h in range(8):
                top16(ca[:, h * 256:(h + 1) * 256], bv[:, h, :], bj8[:, h, :])
            io = CW[:, INV + 64:INV + 80]
            for s in range(2):
                if s == 0:
                    V.then(lambda e: e.tensor_scalar(bh, bj, 4, None, ALU.logical_shift_right))
                else:
                    V.then(lambda e: e.tensor_scalar(bh, bj, 15, None, ALU.bitwise_and))
                vcopy(fa, bh)
                for h in range(8):
                    fh = fa[:, h * 16:(h + 1) * 16].unsqueeze(2).to_broadcast([128, 16, 16])
                    V.do(lambda e, h=h, fh=fh: e.tensor_tensor(oh[:, h, :, :], fh, io.unsqueeze(1).to_broadcast([128, 16, 16]),
                                                               ALU.is_equal), V.now() if h == 0 else None)
                tt(oh, oh, f0[:, :, s, :].unsqueeze(2).to_broadcast([128, 8, 16, 16]), ALU.mult)
                red(fi[s].rearrange("p (h k) -> p h k", h=8), oh, ALU.add)
            stt(fa, fi[0], 128.0, fi[1], ALU.mult, ALU.add)
            mi = vcopy(ix[:, t, :], fa)
            c3 = co[:, t, :].rearrange("p (h k) -> p h k", h=8)
            m = tt(c3, bv, bv[:, :, 0:1].to_broadcast([128, 8, 16]), ALU.subtract)
            m = act(co[:, t, :], co[:, t, :], ACT.Exp, m)
            red(ss[:, 0:8], c3, ALU.add, m)
            recip(ss[:, 0:8], ss[:, 0:8])
            tt(c3, c3, ss[:, 0:8].unsqueeze(2).to_broadcast([128, 8, 16]), ALU.mult)
            return mi

        NG = 12
        Pf = P[:, :, :].rearrange("p t n -> p (t n)")
        gs = [ring[:, j, :] for j in range(7)] + [Pf[:, 4096 + j * 2048:4096 + (j + 1) * 2048] for j in range(5)]
        g_sem = [sem(f"s_g{j}") for j in range(NG)]
        g_cnt = [[0] for _ in range(NG)]
        g_free = [None] * NG
        gn = [0]

        def gather(tab, t, j, mi):
            i = gn[0] % NG
            gn[0] += 1
            return gs[i], G.dma(g_sem[i], g_cnt[i], lambda e: e.indirect_dma_start(
                gs[i], None, tab[0], bass.IndirectOffsetOnAxis(ap=ix[:, t, j:j + 1], axis=0)), mi, g_free[i]), i

        def dots(t, mi):
            for j in range(128):
                u, m, i = gather(I["peer_u_2"], t, j, mi)
                g_free[i] = V.do(lambda e, u=u, j=j: e.tensor_tensor_reduce(
                    out=u, in0=u, in1=hn[t], scale=1.0, scalar=0.0, op0=ALU.mult, op1=ALU.add,
                    accum_out=aa[:, t, j:j + 1]), m, V.now() if j == 0 else None)

        def mix(t, mi):
            for j in range(128):
                v, m, i = gather(I["peer_v_2"], t, j, mi)
                g_free[i] = V.then(lambda e, v=v, j=j: e.scalar_tensor_tensor(
                    out=x[:, t, :], in0=v, scalar=co[:, t, j:j + 1], in1=x[:, t, :], op0=ALU.mult, op1=ALU.add), m)

        G.wait(T.now(), V.now(), A.now())
        mi = [choose(0)]
        G.wait(T.now())
        dots(0, mi[0])
        mi.append(choose(1))
        dots(1, mi[1])
        for t in range(2):
            m = act(aa[:, t, :], aa[:, t, :], ACT.Gelu, V.now())
            tt(co[:, t, :], co[:, t, :], aa[:, t, :], ALU.mult, m)
        o_d = out.rearrange("a (t p) d -> (a p) t d", p=128)
        for t in range(2):
            mix(t, mi[t])
            m = S_.dma(s_o, s_on, lambda e, t=t: e.dma_start(o_d[:, t, :], x[:, t, :]), V.now())
        S_.wait(m)

        block = ctx.enter_context(nc.Block())
        for lane, deco in ((S_, block.sync), (A, block.scalar), (V, block.vector), (G, block.gpsimd), (T, block.tensor)):
            def run(e, lane=lane):
                for f in lane.q:
                    f(e)
            deco(run)


_INS = ["x", "c", "positions", "rel_bias", "norm_gain", "w_mod", "b_mod", "w_in", "q_norm_gain", "k_norm_gain",
        "ret_norm_gain", "w_out", "meta_tokens_2", "norm_mix_2", "w_in_2", "b_forget_2", "fox_q_gain_2",
        "fox_k_gain_2", "sb_out_gain_2", "fox_out_gain_2", "w_out_2", "norm_ffn_2", "peer_w_query_2",
        "peer_sub_keys_2", "peer_u_2", "peer_v_2"]


def kernel(**inputs):
    import concourse.bacc as _bacc
    from concourse import mybir as _mybir
    from concourse.bass_utils import run_bass_kernel_spmd as _run

    nc = _bacc.Bacc("TRN2", target_bir_lowering=False, num_devices=1)
    arrays, args = {}, {}
    cw, dm = constants()
    given = {name: np.ascontiguousarray(inputs[name]) for name in _INS}
    given["cw"], given["dm"] = cw, dm
    for name, a in given.items():
        arrays[f"in_{name}"] = a
        args[name] = nc.dram_tensor(f"in_{name}", a.shape, _mybir.dt.from_np(a.dtype), kind="ExternalInput").ap()
    o = nc.dram_tensor("out_0", (1, 256, 2048), F32, kind="ExternalOutput").ap()
    mixer_peer_program(nc, args, o)
    r = _run(nc, [arrays], core_ids=[0])
    return r.results[0]["out_0"]
```

```python
from contextlib import ExitStack

import numpy as np

import concourse.bass as bass
from concourse import mybir

ALU = mybir.AluOpType
ACT = mybir.ActivationFunctionType
F32 = mybir.dt.float32
FR = mybir.dt.float32r
BF = mybir.dt.bfloat16
I32 = mybir.dt.int32
U32 = mybir.dt.uint32
AX = mybir.AxisListType.X

D = 2048
NK = 16
EPS = 1e-6
NEGV = -1.0e30
TAKEN = -3.0e38
SC = 128.0 ** -0.5

QA, KA, VA, GA, QI, KI, WI, QB, KB, VB, GB = (0, 1024, 1152, 1280, 2304, 3328, 3392, 3408, 4432, 5456, 6480)
GBP, FHP = (QI, 6144)
NP = 6488
SQ, SK, SV, FQ, FK, FV, FG, FL = (0, 1024, 2048, 3072, 4096, 5120, 6144, 7168)
MSK, MSV, MFK, MFV, MFL = (0, 1024, 2048, 3072, 4096)

ID, ONE, TRL, TRU, NTT, SM, NSM, INV, CUT, SEL, ROW, NCW = (0, 128, 256, 384, 512, 640, 768, 896, 976, 980, 996, 1000)
ROWS1 = [("c", 16), ("norm_gain", 32), ("norm_mix_2", 16), ("q_norm_gain", 2), ("k_norm_gain", 2),
         ("fox_q_gain_2", 1), ("fox_k_gain_2", 1), ("ret_norm_gain", 16), ("sb_out_gain_2", 8),
         ("fox_out_gain_2", 8)]


def constants():
    i = np.arange(128)
    cw = np.zeros((128, NCW), np.float32)
    cw[:, ID:ID + 128] = np.eye(128)
    cw[:, ONE:ONE + 128] = 1.0
    cw[:, TRL:TRL + 128] = i[:, None] >= i[None, :]
    cw[:, TRU:TRU + 128] = i[:, None] <= i[None, :]
    cw[:, NTT:NTT + 128] = np.where(i[None, :] > i[:, None], NEGV, 0.0)
    cw[:, SM:SM + 128] = i[None, :] > i[:, None]
    cw[:, NSM:NSM + 128] = np.where(i[None, :] > i[:, None], 0.0, NEGV)
    inv = np.float32(10000.0) ** (-np.arange(64, dtype=np.float32) / np.float32(64))
    cw[:, INV:INV + 64] = inv.astype(np.float32)[None, :]
    cw[:, INV + 64:INV + 80] = np.arange(16)[None, :]
    cut = [-1.0e30] + [float(j) for j in range(1, 17)] + [float(np.ceil(16 * 8 ** (j / 16))) for j in range(1, 16)]
    cw[:, CUT] = np.tile(np.array(cut, np.float32), 4)
    cw[:, SEL:SEL + 16] = (i[:, None] % 32) == 16 + np.arange(16)[None, :]
    cw[:, ROW] = (i % 32) == 0
    lg = np.log1p(-np.exp2(-5.0 - np.arange(8)))
    j, t = np.arange(256)[:, None], np.arange(256)[None, :]
    dm = np.zeros((128, 8, 384), np.float32)
    for h in range(8):
        full = np.where(t >= j, np.exp(lg[h] * np.maximum(t - j, 0)), 0.0)
        dm[:, h, 0:256] = full[0:128]
        dm[:, h, 256:384] = full[128:256, 128:256]
    return cw, dm


class Lane:

    def __init__(self, sem):
        self.sem, self.n, self.q, self.seen = sem, 0, [], {}

    def now(self):
        return (self.sem, self.n)

    def wait(self, *marks):
        for m in marks:
            if m is None or m[1] == 0 or self.seen.get(id(m[0]), 0) >= m[1]:
                continue
            self.seen[id(m[0])] = m[1]
            self.q.append(lambda e, m=m: e.wait_ge(m[0], m[1]))

    def do(self, fn, *marks):
        self.wait(*marks)
        self.n += 1
        self.q.append(lambda e, fn=fn: fn(e).then_inc(self.sem, 1))
        return self.now()

    def then(self, fn, *marks):
        return self.do(fn, *marks, self.now())

    def plain(self, fn, *marks):
        self.wait(*marks)
        self.q.append(fn)

    def dma(self, sem, cnt, fn, *marks):
        self.wait(*marks)
        cnt[0] += 16
        self.q.append(lambda e, fn=fn: fn(e).then_inc(sem, 16))
        return (sem, cnt[0])


def mixer_peer_program(nc, I, out):
    with ExitStack() as ctx:
        def sb(name, shape, dt=F32):
            return ctx.enter_context(nc.sbuf_tensor(name, shape, dt))

        def sem(name):
            return ctx.enter_context(nc.semaphore(name))

        V, A, T, G, S_ = (Lane(sem("l_" + n)) for n in ("v", "a", "t", "g", "s"))

        NS, NB = 4, 3
        x = sb("x", [128, 2, D])
        hH = sb("hH", [128, NK, 256], FR)
        hL = sb("hL", [128, NK, 256], FR)
        hM = sb("hM", [128, NK, 32])
        P = sb("P", [128, 2, NP])
        ring = sb("ring", [128, NS, 1024])
        wH = [sb(f"wH{j}", [128, 1024], FR) for j in range(NB)]
        wL = [sb(f"wL{j}", [128, 1024], FR) for j in range(NB)]
        U = sb("U", [128, 4104])
        TAB = sb("TAB", [128, 4224])
        S = sb("S", [128, 2560])
        SY = sb("SY", [128, 2560])
        CW = sb("CW", [128, NCW])
        cols = sb("cols", [128, 102])
        bcol = sb("bcol", [128, 96])
        cact = sb("cact", [128, 16])
        cs = sb("cs", [128, 2, 2, 64])
        mcol = sb("mcol", [128, 2, 48])
        mrow = sb("mrow", [128, 48])
        msum = sb("msum", [128, 512])
        MI = sb("MI", [128, 1408])
        KIT = MI[:, 0:512].rearrange("p (a n) -> p a n", a=2)
        KAT, IW, NEG = MI[:, 512:768], MI[:, 768:1024], MI[:, 1024:1408]
        sm = sb("sm", [128, 88])
        smy = sb("smy", [128, 72])
        lf = sb("lf", [128, 3, 8])
        fcol = sb("fcol", [128, 2, 8])
        ident = CW[:, ID:ID + 128]
        ones = CW[:, ONE:ONE + 128]

        pp = [ctx.enter_context(nc.psum_tensor(f"pp{i}", [128, 512], F32)) for i in range(4)]
        side_bank, side_free = pp[3], [None]
        tp = [ctx.enter_context(nc.psum_tensor(f"tp{i}", [128, 1024], F32)) for i in range(2)]
        pp_free = [None] * 3
        tp_free = [[], []]
        tpn = [0]

        def pair():
            i = tpn[0] % 2
            tpn[0] += 1
            T.wait(*tp_free[i])
            return tp[i], i

        r_sem = [sem(f"s_r{i}") for i in range(NS)]
        r_cnt = [[0] for _ in range(NS)]
        r_free = [[] for _ in range(NS)]
        rn = [0]
        s_c, s_cn = sem("s_c"), [0]
        s_d, s_dn = sem("s_d"), [0]
        s_m, s_mn = [sem(f"s_m{j}") for j in range(3)], [[0], [0], [0]]
        s_o, s_on = sem("s_o"), [0]

        def load(src, shape):
            i = rn[0] % NS
            rn[0] += 1
            a, b = shape
            v = ring[:, i, 0:a * b].rearrange("p (a b) -> p a b", a=a)
            m = S_.dma(r_sem[i], r_cnt[i], lambda e: e.dma_start(v, src), *r_free[i])
            return v, m, i

        def mm(o, l, r, start, stop, *marks, skip=False, last=False):
            f = lambda e: e.matmul(o, l, r, start=start, stop=stop, skip_group_check=skip)
            if last:
                return T.do(f, *marks)
            T.plain(f, *marks)

        def tr(o, i, *marks, last=False, k=128):
            f = lambda e: e.transpose(o, i, ident[0:k, 0:k])
            if last:
                return T.do(f, *marks)
            T.plain(f, *marks)

        todo, other, side = [], [], []

        def step(q):
            while q:
                try:
                    next(q[0])
                    return
                except StopIteration:
                    q.pop(0)

        owed = [0.0, 0.0, 0.0]

        def pump(rates):
            for k, q in ((0, todo), (1, other), (2, side)):
                owed[k] += rates[k]
                while owed[k] >= 1:
                    step(q)
                    owed[k] -= 1

        def drain(q):
            while q:
                step(q)

        def act(o, i, f, *marks, **kw):
            return A.then(lambda e: e.activation(o, i, f, **kw), *marks)

        def tt(o, a, b, op, *marks):
            return V.then(lambda e: e.tensor_tensor(o, a, b, op), *marks)

        def ts(o, a, s1, s2, op0, op1, *marks):
            if s2 is None:
                return V.then(lambda e: e.tensor_scalar(o, a, s1, None, op0), *marks)
            return V.then(lambda e: e.tensor_scalar(o, a, s1, s2, op0, op1), *marks)

        def stt(o, a, s, b, op0, op1, *marks):
            return V.then(lambda e: e.scalar_tensor_tensor(out=o, in0=a, scalar=s, in1=b, op0=op0, op1=op1), *marks)

        def red(o, i, op, *marks):
            return V.then(lambda e: e.tensor_reduce(o, i, AX, op), *marks)

        def vcopy(o, i, *marks):
            return V.then(lambda e: e.tensor_copy(o, i), *marks)

        def recip(o, i, *marks):
            return V.then(lambda e: e.reciprocal(o, i), *marks)

        def rstd(o, ss, n, t1, t2, *marks):
            ts(t1, ss, 1.0 / n, EPS, ALU.mult, ALU.add, *marks)
            ts(o.bitcast(I32), t1.bitcast(I32), -0.5, 1597463007.0, ALU.mult, ALU.add)
            for _ in range(3):
                tt(t2, o, o, ALU.mult)
                stt(t2, t2, -0.5, t1, ALU.mult, ALU.mult)
                m = stt(o, t2, 1.5, o, ALU.add, ALU.mult)
            return m

        x_d = I["x"].rearrange("a (t p) d -> (a p) t d", p=128)
        A.dma(s_c, s_cn, lambda e: e.dma_start(CW[:, :], I["cw"]))
        stk = S[:, 0:128]
        stk2 = S[:, 128:256]
        r0 = 0
        for nm, nr in ROWS1:
            ap = I[nm]
            src = (ap if len(ap.shape) == 2 else ap.rearrange("(a n) -> a n", a=1)).rearrange("a (k p) -> (a k) p", p=128)
            A.dma(s_c, s_cn, lambda e, r=r0, n=nr, s=src: e.dma_start(stk[r:r + n, :], s))
            r0 += nr
        c_in = A.dma(s_c, s_cn, lambda e: e.dma_start(stk2[0:96, :], I["b_mod"].rearrange("a (k p) -> (a k) p", p=128)))
        posr = S[:, 1256:1512].bitcast(I32)
        posc = S[:, 1512:1514].bitcast(I32)
        poss = S[:, 1516:1580].bitcast(I32)
        rb, rb0 = S[:, 1584:1616], S[:, 1616:1648]
        G.dma(s_d, s_dn, lambda e: e.dma_start(posr, I["positions"][0, :].partition_broadcast(128)))
        for t in range(2):
            G.dma(s_d, s_dn, lambda e, t=t: e.dma_start(
                posc[:, t:t + 1], I["positions"][0, t * 128:(t + 1) * 128].rearrange("(p a) -> p a", a=1)))
        mz = V.then(lambda e: e.memset(S[:, 1584:1648], 0.0))
        for q in range(4):
            G.dma(s_d, s_dn, lambda e, q=q: e.dma_start(
                poss[32 * q:32 * q + 32, :], I["positions"][0, 64 * q:64 * q + 64].partition_broadcast(32)))
            G.dma(s_d, s_dn, lambda e, q=q: e.dma_start(
                rb[32 * q:32 * q + 32, 8 * q:8 * q + 8], I["rel_bias"]), mz)
            G.dma(s_d, s_dn, lambda e, q=q: e.dma_start(
                rb0[32 * q + 1:32 * q + 32, 8 * q:8 * q + 8], I["rel_bias"][0:31, :]))
        p_in = s_d, s_dn[0]
        x_in = G.dma(s_m[0], s_mn[0], lambda e: e.dma_start(x[:, :, :], x_d))
        pr, i = pair()
        tr(pr[:, 0:102], stk[0:102, :], c_in, k=102)
        m = tr(pr[:, 512:608], stk2[0:96, :], last=True, k=96)
        vcopy(cols[:, :], pr[:, 0:102], m)
        c_col = vcopy(bcol[:, :], pr[:, 512:608])
        tp_free[i] = [c_col]
        off, o = {}, 0
        for nm, nr in ROWS1:
            off[nm] = o
            o += nr

        def col(nm, k=0, n=1):
            return cols[:, off[nm] + k:off[nm] + k + n]

        m = act(cact[:, :], col("c", 0, 16), ACT.Exp, c_col, scale=-1.0)
        ts(cact[:, :], cact[:, :], 1.0, None, ALU.add, None, m)
        recip(cact[:, :], cact[:, :])
        c_act = tt(cact[:, :], cact[:, :], col("c", 0, 16), ALU.mult)

        cs_done, qi_read = [None], [None]

        def tables():
            pf = S[:, 1648:1650]
            pk = S[:, 1652:1908]
            ang = S[:, 1908:2036]
            kf = S[:, 2036:2164]
            ki = S[:, 2164:2292].bitcast(I32)
            vcopy(pf, posc, p_in)
            vcopy(pk, posr)
            TP = 6.283185307179586
            C1 = 6.28125
            C2 = float(np.float32(TP - C1))
            C2 = float(np.float32(np.round(C2 * 2 ** 21) / 2 ** 21))
            C3 = float(TP - C1 - C2)
            a2 = ang.rearrange("p (t n) -> p t n", t=2)
            for t in range(2):
                ts(a2[:, t, :], CW[:, INV:INV + 64], pf[:, t:t + 1], None, ALU.mult, None)
            for w in (1, 0):
                ts(kf, ang, 1.0 / TP, 0.25 * (1 - w), ALU.mult, ALU.add)
                vcopy(ki, kf)
                vcopy(kf, ki)
                r = cs[:, w, :, :].rearrange("p t n -> p (t n)")
                stt(r, kf, -C1, ang, ALU.mult, ALU.add)
                stt(r, kf, -C2, r, ALU.mult, ALU.add)
                stt(r, kf, -C3, r, ALU.mult, ALU.add)
                if w == 0:
                    ts(r, r, 0.5 * np.pi, None, ALU.add, None)
                m = ts(r, r, 3.1415925, -3.1415925, ALU.min, ALU.max)
                cs_done[0] = act(r, r, ACT.Sin, m)
            psf = S[:, 2292:2356]
            vcopy(psf, poss)
            tt(rb, rb, rb0, ALU.subtract)
            rp = P[:, 0, 4096:4160].bitcast(BF)
            for k in range(3):
                vcopy(rp[:, k * 32:(k + 1) * 32], rb)
                if k < 2:
                    tt(rb, rb, rp[:, k * 32:(k + 1) * 32], ALU.subtract)
            yield
            hit_read = [None, None]
            for t in range(2):
                for half in range(2):
                    hv = P[:, half, 2048:4096].bitcast(BF).rearrange("p (i q) -> p i q", q=128)
                    mh = stt(hv, pk[:, t * 128:(t + 1) * 128].unsqueeze(1).to_broadcast([128, 32, 128]),
                             CW[:, CUT:CUT + 1],
                             psf[:, half * 32:(half + 1) * 32].unsqueeze(2).to_broadcast([128, 32, 128]),
                             ALU.subtract, ALU.is_ge, hit_read[half])
                    yield
                    for part in range(2):
                        pr = pp[part]
                        for k in range(16 * part, 16 * part + 16):
                            o = (k % 16) * 32
                            for b in range(3):
                                m = mm(pr[:, o:o + 32], hv[:, k, :], rp[:, b * 32:(b + 1) * 32], b == 0, b == 2,
                                       mh, pp_free[part], last=(k % 8 == 7 and b == 2))
                            if k % 16 == 7:
                                yield
                        pv = pr[:, :].rearrange("p (i q h) -> p q h i", q=4, h=8)
                        for q in range(2 if t == 0 else 4):
                            o, n = (0, 128) if t == 0 else (1024, 256)
                            uv = U[:, o:o + 8 * n].rearrange("p (h n) -> p h n", h=8)
                            k0 = 64 * q + 32 * half + 16 * part
                            pp_free[part] = act(uv[:, :, k0:k0 + 16], pv[:, q, :, :], ACT.Copy, m)
                        hit_read[half] = RX.pe = RY.pe = m
                        yield

        mod_ready = {}

        def mod_done(l, g0, g1):
            mc = mcol[:, l, 4 * g0:4 * g1]
            tt(mc, mrow[:, 4 * g0:4 * g1], bcol[:, l * 48 + 4 * g0:l * 48 + 4 * g1], ALU.add)
            if g1 == 8:
                sc_ = mcol[:, l, 16:32]
                ts(sc_, sc_, 1.0, None, ALU.add, None)
                tt(sc_, sc_, col("norm_gain", 16 * l, 16), ALU.mult)
            mod_ready[l, g1] = V.now()

        msum_pe = [None]

        def mod_group(l, g):
            for pc in range(8):
                w, m, i = load(I["w_mod"][l, pc * 256:(pc + 1) * 256, g * 512:(g + 1) * 512]
                               .rearrange("(k p) n -> p k n", p=128), (2, 512))
                for k in range(2):
                    kk = 2 * pc + k
                    q = 32 * (kk % 4)
                    fin = mm(side_bank[q:q + 32, :], cact[:, kk:kk + 1].to_broadcast([128, 32]), w[:, k, :],
                             kk < 4, kk >= 12, m, c_act, side_free[0] if pc == 0 else None, last=(k == 1))
                r_free[i] = [fin]
                if pc < 7:
                    yield
            mc = side_free[0] = act(msum[:, :], side_bank[:, :], ACT.Copy, fin, msum_pe[0])
            yield
            pr, i = pair()
            for b in range(4):
                m = mm(pr[:, b:b + 1], msum[:, b * 128:(b + 1) * 128], CW[:, ROW:ROW + 1], True, True, mc, last=(b == 3))
            msum_pe[0] = m
            tp_free[i] = [vcopy(mrow[:, 4 * g:4 * g + 4], pr[:, 0:4], m)]

        def mods(l, g0, g1):
            for g in range(g0, g1):
                yield from mod_group(l, g)
            mod_done(l, g0, g1)

        class Room:

            def __init__(self, s, small, half):
                self.S, self.H = s, half
                self.ss = small[:, 0:24]
                self.q1, self.q2, self.q3 = (small[:, 24 + 8 * j:32 + 8 * j] for j in range(3))
                self.mx, self.rs, self.m8 = small[:, 48:56], small[:, 56:64], small[:, 64:72]
                self.pe = self.act = self.vec = self.done = None

        RX = Room(S, sm, TAB[:, 0:2112])
        RY = Room(SY, smy, TAB[:, 2112:4224])
        ss, q1, q2, q3 = RX.ss, RX.q1, RX.q2, RX.q3

        def row_norm(meta, squared=True, copied=True):
            if meta:
                V.then(lambda e: e.memset(ss[:, 2:3], 0.0))
            A.wait(V.now(), T.now())
            if not squared:
                for t in range(2):
                    act(P[:, t, 0:D], x[:, t, :], ACT.Square, accum_out=ss[:, t:t + 1])
            else:
                for t in range(2):
                    red(ss[:, t:t + 1], ss[:, 8 + 4 * t:12 + 4 * t], ALU.add, A.now())
            n = 2
            if meta:
                act(P[0:16, 1, D:2 * D], P[0:16, 0, D:2 * D], ACT.Square, s_meta, accum_out=ss[0:16, 2:3])
                n = 3
            m = rstd(q1[:, 0:n], ss[:, 0:n], D, q2[:, 0:n], q3[:, 0:n], A.now())
            if not copied:
                return m
            m2 = [ts(P[:, 1, 0:D], x[:, 1, :], q1[:, 1:2], None, ALU.mult, None, T.now()),
                  act(P[:, 0, 0:D], x[:, 0, :], ACT.Copy, m, scale=q1[:, 0:1])]
            if meta:
                m2.append(act(P[0:16, 1, D:2 * D], P[0:16, 0, D:2 * D], ACT.Copy, scale=q1[0:16, 2:3]))
            return m2

        def to_h(src, ready, ev):
            for k0 in range(0, NK, 4):
                R = (RX, RY)[k0 // 4 % 2]
                tmp = R.S[:, 0:1024]
                pr, i = pair()
                for k in range(k0, k0 + 4):
                    for t in range(2):
                        o = (k - k0) * 256 + t * 128
                        m = tr(pr[:, o:o + 128], src(t, k), *ready, last=(k == k0 + 3 and t == 1))
                for k in range(k0, k0 + 4):
                    e = ev(k, tmp[:, (k - k0) * 256:(k - k0 + 1) * 256], pr[:, (k - k0) * 256:(k - k0 + 1) * 256], m,
                           R.pe, R.act, R.vec)
                tp_free[i] = [e]
                th = tmp.rearrange("p (k n) -> p k n", k=4)
                mh = A.then(lambda e_, k0=k0, th=th: e_.activation(hH[:, k0:k0 + 4, :], th, ACT.Copy), e)
                ml = V.do(lambda e_, k0=k0, th=th: e_.tensor_tensor(hL[:, k0:k0 + 4, :], th, hH[:, k0:k0 + 4, :].bitcast(F32),
                                                               ALU.subtract), mh)
                R.act, R.vec = mh, ml
                yield ml

        w_n = [0]
        w_free = [None] * NB

        def split(wd, c0, w, pc):
            raw, m, i = load(wd[pc * 256:(pc + 1) * 256, c0:c0 + w].rearrange("(k p) n -> p k n", p=128), (2, w))
            j = w_n[0] % NB
            w_n[0] += 1
            hi, lo = (b[j][:, 0:2 * w].rearrange("p (k n) -> p k n", k=2) for b in (wH, wL))
            mh = A.do(lambda e: e.activation(hi, raw, ACT.Copy), m, w_free[j])
            ml = V.do(lambda e: e.tensor_tensor(lo, raw, hi.bitcast(F32), ALU.subtract), mh, w_free[j])
            r_free[i] = [ml]
            return raw, hi, lo, m, ml, i, j

        def three(o, l, r, first, final, *marks, skip=False, last=False):
            mm(o, l[0], r[0], first, False, *marks, skip=skip)
            mm(o, l[0], r[1], False, False, skip=skip)
            return mm(o, l[1], r[0], False, final, skip=skip, last=last)

        ahead, asked = [], [0]

        def begin(wd, groups):
            asked[0] = 0
            for pc in range(NB - 1):
                ahead.append(split(wd, *groups[0], pc))
                asked[0] += 1

        def feed(h, parts, pc):
            if not parts:
                parts.append(next(h))
            if pc % 2 == 0 and pc < 6 and len(parts) < pc // 2 + 2:
                parts.append(next(h))
            return parts[pc // 2]

        def project(wd, groups, h, store, after=None, meta=None, rates=lambda n: (1, 1, 1)):
            pieces = [(n, c0, w, pc) for n, (c0, w) in enumerate(groups) for pc in range(8)]
            parts = []
            for q, (n, c0, w, pc) in enumerate(pieces):
                while asked[0] < min(q + NB, len(pieces)):
                    ahead.append(split(wd, *pieces[asked[0]][1:]))
                    asked[0] += 1
                raw, hi, lo, m, ml, i, j = ahead.pop(0)
                ready_h = feed(h, parts, pc)
                bk = [(2 * n) % 3, (2 * n + 1) % 3]
                md = meta(c0, w) if meta else None
                for t in range(2):
                    for k in range(2):
                        kk = pc * 2 + k
                        hs = hH[:, kk, t * 128:(t + 1) * 128], hL[:, kk, t * 128:(t + 1) * 128]
                        fin = three(pp[bk[t]][:, 0:w], hs, (hi[:, k, :], lo[:, k, :]), kk == 0, kk == 15,
                                    ml, ready_h, pp_free[bk[t]] if kk == 0 else None, last=(k == 1))
                    if pc == 7:
                        pp_free[bk[t]] = store(n, c0, w, t, pp[bk[t]][:, 0:w], fin)
                w_free[j] = fin
                if md:
                    o, dst = md
                    for k in range(2):
                        kk = pc * 2 + k
                        fin = mm(side_bank[32 * (kk % 4):32 * (kk % 4) + 32, 0:w - o], hM[:, kk, :], raw[:, k, o:w],
                                 kk < 4, kk >= 12, m, side_free[0] if pc == 0 else None, last=(k == 1))
                    r_free[i] = r_free[i] + [fin]
                    if pc == 7:
                        side.append(meta_sum(dst, w - o, fin))
                if pc == 7 and after:
                    after(n)
                pump(rates(n))

        def meta_sum(dst, n, fin):
            side_free[0] = mc = act(msum[:, 0:n], side_bank[:, 0:n], ACT.Copy, fin, msum_pe[0])
            yield
            pr, i = pair()
            m = msum_pe[0] = mm(pr[0:16, 0:n], CW[:, SEL:SEL + 16], msum[:, 0:n], True, True, mc, last=True)
            tp_free[i] = [act(dst, pr[0:16, 0:n], ACT.Copy, m)]
            evac[0] = A.now()

        evac = [None]

        def head_rms(R, v, nh, p, *marks):
            m = act(R.S[0:p, 0:nh * 128], v, ACT.Square, R.pe, V.now(), *marks)
            red(R.ss[0:p, 0:nh], R.S[0:p, 0:nh * 128].rearrange("p (h d) -> p h d", h=nh), ALU.add, m)
            R.act = m
            yield
            m = rstd(R.q1[0:p, 0:nh], R.ss[0:p, 0:nh], 128, R.q2[0:p, 0:nh], R.q3[0:p, 0:nh])
            for h in range(nh):
                hv = v[:, h * 128:(h + 1) * 128]
                R.done = A.do(lambda e, h=h, hv=hv: e.activation(hv, hv, ACT.Copy, scale=R.q1[0:p, h:h + 1]), m)
            yield

        def gate(R, g0, y0):
            for t in range(2):
                y = P[:, t, y0:y0 + 1024]
                tt(y, y, P[:, t, g0:g0 + 1024], ALU.mult, R.done)
                yield

        def store_gate(p0, w, t, ps, m, silu, over=None, at=None):
            g = P[:, t, p0:p0 + w] if p0 is not None else at
            m = act(g, ps, ACT.Exp, m, over, scale=-1.0)
            ts(g, g, 1.0, None, ALU.add, None, m)
            m = recip(g, g)
            return tt(g, g, ps, ALU.mult) if silu else m

        def turn_heads(R, src, dst, nh, ready, **kw):
            for h0 in range(0, nh, 4):
                n = min(4, nh - h0)
                pr, i = pair()
                for h in range(n):
                    for t in range(2):
                        o = h * 256 + t * 128
                        m = tr(pr[:, o:o + 128], src(t, h0 + h), ready, last=(h == n - 1 and t == 1))
                r = act(dst[:, h0:h0 + n, :], pr[:, 0:n * 256].rearrange("p (h n) -> p h n", h=n), ACT.Copy,
                        m, R.pe, **kw)
                tp_free[i] = [r]
                yield r

        def sparse(l, ready):
            R, S, mx, rs, m8 = RX, RX.S, RX.mx, RX.rs, RX.m8
            TA = R.H[:, 0:2048].rearrange("p (h n) -> p h n", h=8)
            V.then(lambda e: e.memset(S[:, 0:512], 0.0), R.pe, R.act)
            for t in range(2):
                ki = P[:, t, KI:KI + 64]
                vcopy(S[:, t * 256:t * 256 + 64], ki, ready[3])
                m = vcopy(S[:, t * 256 + 192:t * 256 + 256], ki)
            pr, i = pair()
            for e_ in range(2):
                for t in range(2):
                    o = e_ * 256 + t * 128
                    mt = tr(pr[:, o:o + 128], S[:, t * 256 + e_ * 128:t * 256 + e_ * 128 + 128], m,
                            last=(e_ == 1 and t == 1))
            mki = vcopy(KIT[:, :, :].rearrange("p a n -> p (a n)"), pr[:, 0:512], mt)
            tp_free[i] = [mki]
            yield
            for mq in turn_heads(R, lambda t, h: P[:, t, QI + h * 128:QI + (h + 1) * 128], TA, 8, ready[3]):
                yield
            qi_read[0] = T.now()
            yield
            for t in range(2):
                nk = 128 * (t + 1)
                used = [V.now(), V.now()]
                for g in range(4):
                    pr, i = pair()
                    for b in range(2):
                        for e_ in range(2):
                            m = mm(pr[:, b * 512 + e_ * nk:b * 512 + (e_ + 1) * nk],
                                   TA[:, 2 * g + b, t * 128:(t + 1) * 128], KIT[:, e_, 0:nk], True, True,
                                   mq, mki, last=(b == 1 and e_ == 1))
                    R.pe = m
                    r = S[:, 512 + (g % 2) * 1024:512 + (g % 2) * 1024 + 4 * nk]
                    mr = act(r.rearrange("p (b n) -> p b n", b=2),
                             pr.rearrange("p (b n) -> p b n", b=2)[:, :, 0:2 * nk], ACT.Relu, m, used[g % 2])
                    tp_free[i] = [mr]
                    R.act = mr
                    for h in range(4):
                        wh = P[:, t, WI + 4 * g + h:WI + 4 * g + h + 1]
                        rh = r[:, h * nk:(h + 1) * nk]
                        if g == 0 and h == 0:
                            ts(IW[:, 0:nk], rh, wh, None, ALU.mult, None, mr)
                        else:
                            used[g % 2] = stt(IW[:, 0:nk], rh, wh, IW[:, 0:nk], ALU.mult, ALU.add, mr)
                    yield
                w = IW[:, 0:nk]
                tt(w[:, nk - 128:nk], w[:, nk - 128:nk], CW[:, NTT:NTT + 128], ALU.add)
                for r_ in range(8):
                    V.then(lambda e, w=w: e.max(m8, w))
                    V.then(lambda e, w=w: e.match_replace(w, m8, w, TAKEN))
                    if r_ % 3 == 2:
                        yield
                ng = NEG[:, t * 128:t * 128 + nk]
                ts(ng, w, -2.0e38, NEGV, ALU.is_gt, ALU.mult)
                tt(ng[:, nk - 128:nk], ng[:, nk - 128:nk], CW[:, NTT:NTT + 128], ALU.add)
                yield
            for t in range(2):
                yield from head_rms(R, P[:, t, QA:QA + 1024], 8, 128, ready[5])
                yield from head_rms(R, P[:, t, KA:KA + 128], 1, 128)
                mk = R.done
            gk = cols[:, off["k_norm_gain"] + l:off["k_norm_gain"] + l + 1]
            gq = cols[:, off["q_norm_gain"] + l:off["q_norm_gain"] + l + 1]
            for _ in turn_heads(R, lambda t, h: P[:, t, KA:KA + 128],
                                KAT[:, :].rearrange("p (a n) -> p a n", a=1), 1, mk, scale=gk):
                pass
            for mq in turn_heads(R, lambda t, h: P[:, t, QA + h * 128:QA + (h + 1) * 128], TA, 8, mk, scale=gq):
                yield
            yield
            for t in range(2):
                nk = 128 * (t + 1)
                for g in range(2):
                    pr, i = pair()
                    for h in range(4):
                        o = (h // 2) * 512 + (h % 2) * nk
                        m = mm(pr[:, o:o + nk], TA[:, 4 * g + h, t * 128:(t + 1) * 128], KAT[:, 0:nk], True, True,
                               mq, last=(h == 3))
                    bo = (0 if t == 0 else 1024) + 4 * g * nk
                    s0 = S[:, 0:4 * nk]
                    tp_free[i] = [stt(s0.rearrange("p (b n) -> p b n", b=2),
                                      pr.rearrange("p (b n) -> p b n", b=2)[:, :, 0:2 * nk], SC,
                                      U[:, bo:bo + 4 * nk].rearrange("p (b n) -> p b n", b=2),
                                      ALU.mult, ALU.add, m, R.pe, R.act)]
                    yield
                    s4 = s0.rearrange("p (h n) -> p h n", h=4)
                    ng = NEG[:, t * 128:t * 128 + nk]
                    tt(s4, s4, ng.unsqueeze(1).to_broadcast([128, 4, nk]), ALU.add)
                    red(mx[:, 0:4], s4, ALU.max)
                    m = ts(mx[:, 0:4], mx[:, 0:4], -1.0, None, ALU.mult, None)
                    for h in range(4):
                        me = A.do(lambda e, h=h, s4=s4: e.activation(
                            s4[:, h, :], s4[:, h, :], ACT.Exp, bias=mx[:, h:h + 1], accum_out=rs[:, h:h + 1]), m)
                    R.act = me
                    yield
                    pr, i = pair()
                    nt = t + 1
                    for h in range(4):
                        for kt in range(nt):
                            o = (h * nt + kt) * 128
                            m = tr(pr[:, o:o + 128], s4[:, h, kt * 128:(kt + 1) * 128], me,
                                   last=(h == 3 and kt == nt - 1))
                    pT = S[:, 1024:1024 + 512 * nt]
                    R.pe = m
                    mp = R.act = act(pT, pr[:, 0:512 * nt], ACT.Copy, m)
                    tp_free[i] = [mp]
                    mrs = recip(rs[:, 0:4], rs[:, 0:4], me)
                    yield
                    pr, i = pair()
                    for h in range(4):
                        for kt in range(nt):
                            o = (h * nt + kt) * 128
                            m = mm(pr[:, h * 128:(h + 1) * 128], pT[:, o:o + 128], P[:, kt, VA:VA + 128],
                                   kt == 0, kt == nt - 1, mp, ready[3], last=(h == 3 and kt == nt - 1))
                    R.pe = m
                    for h in range(4):
                        o = QA + (4 * g + h) * 128
                        R.done = A.do(lambda e, h=h, o=o, t=t, pr=pr: e.activation(
                            P[:, t, o:o + 128], pr[:, h * 128:(h + 1) * 128], ACT.Copy, scale=rs[:, h:h + 1]), m, mrs)
                    tp_free[i] = [R.done]
                    yield

        dm_free = [None]

        def retention(half, ready):
            R, S = RY, RY.S
            rd = ready[8 + 3 * half]
            for c0 in (QB, KB):
                for t in range(2):
                    v = P[:, t, c0 + 512 * half:c0 + 512 * half + 512].rearrange("p (h d) -> p h d", h=4)
                    x1, x2 = v[:, :, 0:64], v[:, :, 64:128]
                    co = cs[:, 0, t, :].unsqueeze(1).to_broadcast([128, 4, 64])
                    si = cs[:, 1, t, :].unsqueeze(1).to_broadcast([128, 4, 64])
                    t1, t2, t3 = (S[:, j * 256:(j + 1) * 256].rearrange("p (h d) -> p h d", h=4) for j in range(3))
                    tt(t1, x1, co, ALU.mult, rd, R.pe, R.act, cs_done[0])
                    tt(t2, x2, si, ALU.mult)
                    tt(t3, x1, si, ALU.mult)
                    tt(x2, x2, co, ALU.mult)
                    tt(x1, t1, t2, ALU.subtract)
                    mr = tt(x2, x2, t3, ALU.add)
                    yield
            TQ = R.H[:, 0:1024].rearrange("p (h n) -> p h n", h=4)
            TK = R.H[:, 1024:2048].rearrange("p (h n) -> p h n", h=4)
            for g in (2 * half, 2 * half + 1):
                if g % 2 == 0:
                    h0 = 2 * g
                    for _ in turn_heads(R, lambda t, h: P[:, t, QB + (h0 + h) * 128:QB + (h0 + h + 1) * 128], TQ, 4, mr):
                        yield
                    for mq in turn_heads(R, lambda t, h: P[:, t, KB + (h0 + h) * 128:KB + (h0 + h + 1) * 128], TK, 4, mr,
                                         scale=SC):
                        yield
                b = g % 2
                dmt = U[:, 3072:3840]
                md = G.dma(s_d, s_dn, lambda e, g=g: e.dma_start(
                    dmt, I["dm"][:, 2 * g:2 * g + 2, :].rearrange("p h n -> p (h n)")), dm_free[0])
                pr, i = pair()
                for h in range(2):
                    hh = 2 * (g % 2) + h
                    mm(pr[:, h * 512:h * 512 + 256], TK[:, hh, 0:128], TQ[:, hh, :], True, True, mq)
                    m = mm(pr[:, h * 512 + 256:h * 512 + 384], TK[:, hh, 128:256], TQ[:, hh, 128:256], True, True,
                           last=True)
                st = S[:, b * 768:(b + 1) * 768].rearrange("p (h n) -> p h n", h=2)
                ms = tt(st, pr.rearrange("p (h n) -> p h n", h=2)[:, :, 0:384],
                        dmt.rearrange("p (h n) -> p h n", h=2), ALU.mult, m, md, R.pe)
                tp_free[i] = [ms]
                dm_free[0] = ms
                yield
                pr, i = pair()
                for h in range(2):
                    vb = VB + (2 * g + h) * 128
                    mm(pr[:, h * 128:(h + 1) * 128], st[:, h, 0:128], P[:, 0, vb:vb + 128], True, True, ms, rd)
                    mm(pr[:, 512 + h * 128:640 + h * 128], st[:, h, 128:256], P[:, 0, vb:vb + 128], True, False)
                    m = mm(pr[:, 512 + h * 128:640 + h * 128], st[:, h, 256:384], P[:, 1, vb:vb + 128], False, True,
                           last=True)
                R.pe = m
                mo = act(P[:, :, QB + g * 256:QB + (g + 1) * 256], pr[:, :].rearrange("p (t n) -> p t n", t=2)[:, :, 0:256],
                         ACT.Copy, m)
                tp_free[i] = [mo]
                yield
            for t in range(2):
                c0 = QB + 512 * half
                v = P[:, t, c0:c0 + 512].rearrange("p (h d) -> p h d", h=4)
                red(R.ss[:, 0:4], v, ALU.add, mo)
                ts(R.ss[:, 0:4], R.ss[:, 0:4], -1.0 / 128, None, ALU.mult, None)
                tt(v, v, R.ss[:, 0:4].unsqueeze(2).to_broadcast([128, 4, 128]), ALU.add)
                yield
                yield from head_rms(R, P[:, t, c0:c0 + 512], 4, 128)

        def cgroups(*spans):
            r = []
            for c0, n, w in spans:
                r += [(c0 + j * w, w) for j in range(n)]
            return r

        def square(n, t, m):
            act(SY[:, t * 512:t * 512 + 512], x[:, t, n * 512:(n + 1) * 512], ACT.Square, m, RY.pe,
                accum_out=ss[:, 8 + 4 * t + n:9 + 4 * t + n])
            RY.act = A.now()

        def store_p(n, c0, w, t, ps, m):
            if GA <= c0 < QI:
                return store_gate(c0, w, t, ps, m, True)
            if c0 >= GB:
                return store_gate(GBP + c0 - GB, w, t, ps, m, True, qi_read[0])
            return act(P[:, t, c0:c0 + w], ps, ACT.Copy, m)

        A.wait(x_in)
        V.wait(x_in)
        early = row_norm(False, squared=False)
        todo.append(tables())
        for k, _ in enumerate(mods(0, 0, 8)):
            if k % 3 == 2:
                step(todo)
        drain(todo)
        side += [mods(0, 8, 12), mods(1, 0, 8), mods(1, 8, 12)]
        for l in range(2):
            m = mod_ready[l, 8]
            begin(I["w_in"][l], [(QI, 368)])
            mn = row_norm(False) if l else early
            ev = lambda k, o, ps, *mk: ts(o, ps, mcol[:, l, 16 + k:17 + k], mcol[:, l, k:k + 1], ALU.mult, ALU.add, *mk)
            h = to_h(lambda t, k: P[:, t, k * 128:(k + 1) * 128], mn, ev)
            groups = cgroups((QI, 3, 368), (KA, 1, 256), (QA, 2, 512), (QB, 1, 512), (KB, 1, 512), (VB, 1, 512),
                             (QB + 512, 1, 512), (KB + 512, 1, 512), (VB + 512, 1, 512), (GA, 2, 512), (GB, 2, 512))

            gb = TAB[:, 0:2048]

            def gate_rows():
                while (l, 12) not in mod_ready:
                    step(side)
                for k0 in range(0, NK, 8):
                    for k in range(k0, k0 + 8):
                        md = ts(S[:, (k - k0) * 128:(k - k0 + 1) * 128], ident, mcol[:, l, 32 + k:33 + k], None,
                                ALU.mult, None, RX.pe, RX.act)
                    yield
                    pr, i = pair()
                    for b in range(2):
                        m = mm(pr[:, b * 512:(b + 1) * 512], ones, S[:, b * 512:(b + 1) * 512], True, True, md, last=True)
                    RX.pe = m
                    tp_free[i] = [vcopy(gb[:, k0 * 128:(k0 + 8) * 128], pr[:, :], m)]
                    yield

            def after(n):
                ready[n] = A.now()
                if n == 3:
                    todo.append(sparse(l, ready))
                if n == 8:
                    other.append(retention(0, ready))
                if n == 11:
                    other.append(retention(1, ready))
                if n == 13:
                    todo.append(gate(RX, GA, QA))
                    todo.append(gate_rows())
                if n == 15:
                    other.append(gate(RY, GBP, QB))

            ready = {}
            project(I["w_in"][l], groups, h, store_p, after,
                    rates=lambda n: (0.7 if n < 14 else 1.0, 0.6, 1.0))
            while todo or other:
                step(todo)
                step(other)
            gr = off["ret_norm_gain"] + 8 * l

            def ev(k, o, ps, *mk):
                if k < 8:
                    return act(o, ps, ACT.Copy, *mk)
                return act(o, ps, ACT.Copy, *mk, scale=cols[:, gr + k - 8:gr + k - 7])

            my = V.now()
            ysrc = lambda t, k: P[:, t, (QA if k < 8 else QB - 1024) + k * 128:(QA if k < 8 else QB - 1024) + (k + 1) * 128]
            begin(I["w_out"][l], [(0, 512)])
            h = to_h(ysrc, [my], ev)

            def store_x(n, c0, w, t, ps, m):
                tmp = S[:, 1024 + t * 512:1024 + (t + 1) * 512]
                r = tt(tmp, ps, gb[:, c0:c0 + w], ALU.mult, m)
                square(n, t, tt(x[:, t, c0:c0 + w], x[:, t, c0:c0 + w], tmp, ALU.add))
                return r

            project(I["w_out"][l], cgroups((0, 4, 512)), h, store_x)
            drain(side)

        PM = U[0:16, 0:4104]
        s_meta = G.dma(s_m[0], s_mn[0], lambda e: e.dma_start(P[0:16, 0, D:2 * D], I["meta_tokens_2"]), V.now(), T.now(), A.now())
        begin(I["w_in_2"][0], [(FG + 688, 344)])
        mn = row_norm(True)
        ev = lambda k, o, ps, *mk: ts(o, ps, col("norm_mix_2", k), None, ALU.mult, None, *mk)
        h = to_h(lambda t, k: P[:, t, k * 128:(k + 1) * 128], mn, ev)
        pr, i = pair()
        for k in range(NK):
            m = tr(pr[:, k * 16:(k + 1) * 16], P[0:16, 1, D + k * 128:D + (k + 1) * 128], mn[2], k=16, last=(k == 15))
        V.then(lambda e: e.memset(hM[:, :, 0:16], 0.0))
        tp_free[i] = [tt(hM[:, :, 16:32], pr[:, 0:256].rearrange("p (k n) -> p k n", k=16),
                         col("norm_mix_2", 0, 16).unsqueeze(2).to_broadcast([128, 16, 16]), ALU.mult, m)]
        bf = sm[:, 72:80]
        m_bf = G.dma(s_m[1], s_mn[1], lambda e: e.dma_start(bf, I["b_forget_2"].rearrange("a h -> (a h)").partition_broadcast(128)))
        A.wait(T.now(), V.now())

        def meta(c0, w):
            for a, b in ((SK, MSK), (SV, MSV), (FK, MFK), (FV, MFV)):
                if a <= c0 < a + 1024:
                    return 0, PM[:, b + c0 - a:b + c0 - a + w]
            if c0 + w > FL:
                return FL - c0, PM[:, MFL:MFL + 8]
            return None

        def turn_keys(R, src, msrc, TB, ready, **kw):
            for mk in turn_heads(R, src, TB[:, :, 16:272], 4, ready, **kw):
                yield mk
            pr, i = pair()
            for h in range(4):
                m = tr(pr[:, h * 16:(h + 1) * 16], msrc(h), k=16, last=(h == 3))
            mk = act(TB[:, :, 0:16], pr[:, 0:64].rearrange("p (h n) -> p h n", h=4), ACT.Copy, m, **kw)
            tp_free[i] = [mk]
            yield mk

        def stick(half, ready):
            R, S = RY, RY.S
            TA = R.H[:, 0:1024].rearrange("p (h n) -> p h n", h=4)
            TB = R.H[:, 1024:2112].rearrange("p (h n) -> p h n", h=4)
            z = S[:, 0:1280].rearrange("p (h n) -> p h n", h=2)
            L = S[:, 1280:2560].rearrange("p (h n) -> p h n", h=2)
            zx, zm = z[:, :, 0:384], z[0:16, :, 384:640]
            Lx, Lm = L[:, :, 0:384], L[0:16, :, 384:640]
            parts = ((zx, Lx), (zm, Lm))
            for g in (2 * half, 2 * half + 1):
                if g % 2 == 0:
                    h0 = 2 * g
                    for _ in turn_heads(R, lambda t, h: P[:, t, SQ + (h0 + h) * 128:SQ + (h0 + h + 1) * 128], TA, 4, ready):
                        yield
                    for mk in turn_keys(R, lambda t, h: P[:, t, SK + (h0 + h) * 128:SK + (h0 + h + 1) * 128],
                                        lambda h: PM[:, MSK + (h0 + h) * 128:MSK + (h0 + h + 1) * 128], TB, ready):
                        yield
                pr, i = pair()
                for h in range(2):
                    hh = 2 * (g % 2) + h
                    mm(pr[:, h * 512:h * 512 + 256], TB[:, hh, 16:144], TA[:, hh, :], True, True, mk)
                    m = mm(pr[:, h * 512 + 256:h * 512 + 384], TB[:, hh, 144:272], TA[:, hh, 128:256], True, True,
                           last=True)
                tp_free[i] = [act(zx, pr.rearrange("p (h n) -> p h n", h=2)[:, :, 0:384], ACT.Copy, m, R.pe, V.now(),
                                  scale=SC)]
                pr, i = pair()
                for h in range(2):
                    m = mm(pr[0:16, h * 256:(h + 1) * 256], TB[:, 2 * (g % 2) + h, 0:16], TA[:, 2 * (g % 2) + h, :], True, True,
                           last=True)
                mz = act(zm, pr[0:16, 0:512].rearrange("p (h n) -> p h n", h=2), ACT.Copy, m, scale=SC)
                tp_free[i] = [mz]
                for a, b in parts:
                    A.do(lambda e, a=a, b=b: e.activation(b, a, ACT.Abs), mz)
                m = A.now()
                for a, b in parts:
                    A.do(lambda e, b=b: e.activation(b, b, ACT.Exp, scale=-1.0), m)
                m = A.now()
                for a, b in parts:
                    A.do(lambda e, b=b: e.activation(b, b, ACT.Ln, bias=1.0), m)
                m = A.now()
                for a, b in parts:
                    stt(b, a, 0.0, b, ALU.max, ALU.add, m)
                yield
                z5, L5 = (S[:, o:o + 1280].rearrange("p (h c n) -> p h c n", h=2, c=5)[:, :, 0:3:2, :] for o in (0, 1280))
                mL = tt(L5, L5, CW[:, SM:SM + 128].unsqueeze(1).unsqueeze(1).to_broadcast([128, 2, 2, 128]), ALU.mult)
                tt(z5, z5, CW[:, NSM:NSM + 128].unsqueeze(1).unsqueeze(1).to_broadcast([128, 2, 2, 128]), ALU.add)
                yield
                pr, i = pair()
                trl = CW[:, TRL:TRL + 128]
                for h in range(2):
                    o = h * 512
                    mm(pr[:, o:o + 256], trl, L[:, h, 0:256], True, False, mL)
                    mm(pr[:, o + 128:o + 256], ones, L[:, h, 256:384], False, True)
                    m = mm(pr[:, o + 256:o + 384], trl, L[:, h, 256:384], True, True, last=True)
                tp_free[i] = [tt(zx, zx, pr.rearrange("p (h n) -> p h n", h=2)[:, :, 0:384], ALU.subtract, m)]
                act(zx, zx, ACT.Exp, V.now())
                pr, i = pair()
                for h in range(2):
                    o = h * 256
                    mm(pr[0:16, o:o + 256], trl[0:16, 0:16], L[0:16, h, 384:640], True, False)
                    mm(pr[0:16, o:o + 256], ones[:, 0:16], L[:, h, 0:256], False, False)
                    m = mm(pr[0:16, o + 128:o + 256], ones[:, 0:16], L[:, h, 256:384], False, True, last=True)
                tp_free[i] = [tt(zm, zm, pr[0:16, 0:512].rearrange("p (h n) -> p h n", h=2), ALU.subtract, m)]
                mw = act(zm, zm, ACT.Exp, V.now())
                R.act = mw
                yield
                pr, i = pair()
                for h in range(2):
                    vc = SV + (2 * g + h) * 128
                    vm = PM[:, MSV + (2 * g + h) * 128:MSV + (2 * g + h + 1) * 128]
                    o = h * 128
                    mm(pr[:, o:o + 128], z[:, h, 0:128], P[:, 0, vc:vc + 128], True, False, mw)
                    mm(pr[:, o:o + 128], z[0:16, h, 384:512], vm, False, True)
                    o += 512
                    mm(pr[:, o:o + 128], z[:, h, 128:256], P[:, 0, vc:vc + 128], True, False)
                    mm(pr[:, o:o + 128], z[:, h, 256:384], P[:, 1, vc:vc + 128], False, False)
                    m = mm(pr[:, o:o + 128], z[0:16, h, 512:640], vm, False, True, last=True)
                R.pe = m
                R.done = act(P[:, :, SQ + g * 256:SQ + (g + 1) * 256], pr[:, :].rearrange("p (t n) -> p t n", t=2)[:, :, 0:256],
                             ACT.Copy, m)
                tp_free[i] = [R.done]
                yield
            if half:
                yield from out_rms(R, SQ)

        def out_rms(R, c0):
            for t in range(2):
                v = P[:, t, c0:c0 + 1024]
                tt(R.S[:, 0:1024], v, v, ALU.mult, R.pe, R.act, R.done)
                yield
                red(R.ss[:, 0:1], R.S[:, 0:1024], ALU.add)
                rstd(R.q1[:, 0:1], R.ss[:, 0:1], 1024, R.q2[:, 0:1], R.q3[:, 0:1])
                ts(v, v, R.q1[:, 0:1], None, ALU.mult, None)
                yield

        mf_done = [None]

        def fox_pair(R, g, TA, TB, mk):
            S, mx, rs = R.S, R.mx, R.rs
            tru = CW[:, TRU:TRU + 128]
            lb = S[:, 1792:2560].rearrange("p (h t n) -> p h t n", h=2, t=3)
            for h in range(2):
                for t in range(3):
                    p = 16 if t == 2 else 128
                    mb = A.do(lambda e, h=h, t=t, p=p, g=g, lb=lb: e.activation(
                        lb[0:p, h, t, :], ones[0:p, :], ACT.Copy, scale=lf[0:p, t, 2 * g + h:2 * g + h + 1]),
                        R.pe, V.now(), mf_done[0])
            for t in range(2):
                nk = 144 + 128 * t
                pr, i = pair()
                for h in range(2):
                    o = h * 512
                    mm(pr[:, o:o + nk], TA[:, 2 * (g % 2) + h, t * 128:(t + 1) * 128], TB[:, 2 * (g % 2) + h, 0:nk], True, False,
                       mk, mb)
                    mm(pr[:, o:o + 16], lb[0:16, h, 2, :], tru[0:16, 0:16], False, False)
                    for c in range(16, nk, 128):
                        mm(pr[:, o + c:o + c + 128], lb[0:16, h, 2, :], ones[0:16, :], False, False)
                    m = mm(pr[:, o + 16:o + 144], lb[:, h, 0, :], tru, False, t == 0, last=True)
                    if t == 1:
                        mm(pr[:, o + 144:o + 272], lb[:, h, 0, :], ones, False, False)
                        m = mm(pr[:, o + 144:o + 272], lb[:, h, 1, :], tru, False, True, last=True)
                R.pe = m
                s = S[:, 0:2 * nk].rearrange("p (h n) -> p h n", h=2)
                tp_free[i] = [act(s, pr.rearrange("p (h n) -> p h n", h=2)[:, :, 0:nk], ACT.Copy, m, V.now(),
                                  scale=SC)]
                dg = s[:, :, nk - 128:nk]
                tt(dg, dg, CW[:, NTT:NTT + 128].unsqueeze(1).to_broadcast([128, 2, 128]), ALU.add, A.now())
                red(mx[:, 0:2], s, ALU.max)
                fc = fcol[:, t, 2 * g:2 * g + 2]
                tt(mx[:, 0:2], mx[:, 0:2], fc, ALU.add)
                m = tt(mx[:, 0:2], fc, mx[:, 0:2], ALU.subtract)
                for h in range(2):
                    me = A.do(lambda e, h=h, s=s: e.activation(
                        s[:, h, :], s[:, h, :], ACT.Exp, bias=mx[:, h:h + 1], accum_out=rs[:, h:h + 1]), m)
                R.act = me
                yield
                pr, i = pair()
                nt = t + 2
                for h in range(2):
                    tr(pr[0:16, h * 512:h * 512 + 128], s[:, h, 0:16], me)
                    for kt in range(1, nt):
                        m = tr(pr[:, h * 512 + kt * 128:h * 512 + (kt + 1) * 128],
                               s[:, h, 16 + (kt - 1) * 128:16 + kt * 128], last=True)
                R.pe = m
                pT = S[:, 1024:1792].rearrange("p (h n) -> p h n", h=2)
                prh = pr.rearrange("p (h n) -> p h n", h=2)
                act(pT[0:16, :, 0:128], prh[0:16, :, 0:128], ACT.Copy, m)
                mp = act(pT[:, :, 128:nt * 128], prh[:, :, 128:nt * 128], ACT.Copy)
                tp_free[i] = [mp]
                mrs = recip(rs[:, 0:2], rs[:, 0:2], me)
                yield
                pr, i = pair()
                for h in range(2):
                    o = h * 128
                    hv = (2 * g + h) * 128
                    mm(pr[:, o:o + 128], pT[0:16, h, 0:128], PM[:, MFV + hv:MFV + hv + 128], True, False, mp)
                    for kt in range(1, nt):
                        m = mm(pr[:, o:o + 128], pT[:, h, kt * 128:(kt + 1) * 128],
                               P[:, kt - 1, FV + hv:FV + hv + 128], False, kt == nt - 1, last=True)
                R.pe = m
                for h in range(2):
                    o = FQ + (2 * g + h) * 128
                    R.done = A.do(lambda e, h=h, o=o, t=t, pr=pr: e.activation(
                        P[:, t, o:o + 128], pr[:, h * 128:(h + 1) * 128], ACT.Copy, scale=rs[:, h:h + 1]), m, mrs)
                tp_free[i] = [R.done]
                yield

        fox_mk = {}

        def fox_turn(half, c0, ready):
            R = RX
            for t in range(2):
                yield from head_rms(R, P[:, t, c0 + 512 * half:c0 + 512 * half + 512], 4, 128, ready)
            h0 = 4 * half
            src = lambda t, h: P[:, t, c0 + (h0 + h) * 128:c0 + (h0 + h + 1) * 128]
            if c0 == FQ:
                TA = R.H[:, 0:1024].rearrange("p (h n) -> p h n", h=4)
                for _ in turn_heads(R, src, TA, 4, R.done, scale=col("fox_q_gain_2")):
                    yield
                return
            yield from head_rms(R, PM[:, MFK + 512 * half:MFK + 512 * half + 512], 4, 16)
            TB = R.H[:, 1024:2112].rearrange("p (h n) -> p h n", h=4)
            for fox_mk[half] in turn_keys(R, src, lambda h: PM[:, MFK + (h0 + h) * 128:MFK + (h0 + h + 1) * 128], TB,
                                          R.done, scale=col("fox_k_gain_2")):
                yield

        def fox(half, ready):
            R, q1 = RX, RX.q1
            TA = R.H[:, 0:1024].rearrange("p (h n) -> p h n", h=4)
            TB = R.H[:, 1024:2112].rearrange("p (h n) -> p h n", h=4)
            tru = CW[:, TRU:TRU + 128]
            if half == 0:
                for t in range(3):
                    p = 16 if t == 2 else 128
                    v = PM[:, MFL:MFL + 8] if t == 2 else P[:, t, FHP + 336:FHP + 344]
                    f, e1 = lf[0:p, t, :], q1[0:p, 0:8]
                    tt(f, v, bf_s[0:p, :], ALU.add, ready)
                    act(e1, f, ACT.Abs, V.now())
                    act(e1, e1, ACT.Exp, scale=-1.0)
                    m = act(e1, e1, ACT.Ln, bias=1.0)
                    stt(f, f, 0.0, e1, ALU.min, ALU.subtract, m)
                mf = V.now()
                pr, i = pair()
                mm(pr[:, 0:8], ones[0:16, :], lf[0:16, 2, :], True, False, mf)
                mm(pr[:, 0:8], tru, lf[:, 0, :], False, True)
                mm(pr[:, 8:16], ones[0:16, :], lf[0:16, 2, :], True, False)
                mm(pr[:, 8:16], ones, lf[:, 0, :], False, False)
                m = mm(pr[:, 8:16], tru, lf[:, 1, :], False, True, last=True)
                tp_free[i] = [vcopy(fcol[:, :, :].rearrange("p t h -> p (t h)"), pr[:, 0:16], m)]
                for t in range(2):
                    ts(lf[:, t, :], lf[:, t, :], -1.0 / SC, None, ALU.mult, None)
                mf_done[0] = ts(lf[0:16, 2, :], lf[0:16, 2, :], -1.0 / SC, None, ALU.mult, None)
                yield
            mk = fox_mk[half]
            for g in (2 * half, 2 * half + 1):
                if half and g == 2:
                    other.append(fox_pair(RY, 3, TA, TB, mk))
                    yield from fox_pair(R, 2, TA, TB, mk)
                    while other:
                        step(other)
                        yield
                    RX.pe, RX.act, RX.done = T.now(), A.now(), A.now()
                    break
                yield from fox_pair(R, g, TA, TB, mk)

        def finish_fox():
            for t in range(2):
                act(RX.S[:, 1024:2048], P[:, t, FQ:FQ + 1024], ACT.Square, RX.pe, RX.done, V.now(), accum_out=RX.ss[:, t:t + 1])
            rstd(RX.q1[:, 0:2], RX.ss[:, 0:2], 1024, RX.q2[:, 0:2], RX.q3[:, 0:2], A.now())
            for t in range(2):
                for y0, g in ((FQ, MI[:, t * 688:(t + 1) * 688]), (FQ + 688, P[:, t, FHP:FHP + 336])):
                    y = P[:, t, y0:y0 + g.shape[1]]
                    stt(y, y, RX.q1[:, t:t + 1], g, ALU.mult, ALU.mult)
            yield

        bf_s = sm[:, 80:88]
        vcopy(bf_s, bf, m_bf)
        halves = [(c + 512 * h, 1, 512) for h in range(2) for c in (SQ, SK, SV, FQ, FK, FV)]
        groups = cgroups((FG + 688, 1, 344), *halves, (FG, 2, 344))

        def store_2(n, c0, w, t, ps, m):
            if c0 == FG + 688:
                r = store_gate(FHP, 336, t, ps[:, 0:336], m, False)
                return act(P[:, t, FHP + 336:FHP + 344], ps[:, 336:344], ACT.Copy, r)
            if c0 >= FG:
                return store_gate(None, w, t, ps, m, False, at=MI[:, t * 688 + c0 - FG:t * 688 + c0 - FG + w])
            return act(P[:, t, c0:c0 + w], ps, ACT.Copy, m)

        def after(n):
            drain(side)
            if n in (3, 9):
                other.append(stick(n // 9, A.now()))
            if n in (4, 5, 10, 11):
                todo.append(fox_turn(n // 10, FQ if n % 6 == 4 else FK, A.now()))
            if n in (6, 12):
                todo.append(fox(n // 12, A.now()))
            if n == 14:
                todo.append(finish_fox())

        T.wait(V.now())
        project(I["w_in_2"][0], groups, h, store_2, after, meta, rates=lambda n: (0.8 if n < 13 else 1, 0.6, 1))
        while todo or other:
            step(todo)
            step(other)
        ysrc = lambda t, k: P[:, t, (SQ if k < 8 else FQ - 1024) + k * 128:(SQ if k < 8 else FQ - 1024) + (k + 1) * 128]
        begin(I["w_out_2"][0], [(0, 512)])
        g0 = off["sb_out_gain_2"]
        ev = lambda k, o, ps, *mk: act(o, ps, ACT.Copy, *mk, scale=cols[:, g0 + k:g0 + k + 1])
        h = to_h(ysrc, [V.now()], ev)

        def store_h(n, c0, w, t, ps, m):
            m = tt(x[:, t, c0:c0 + w], x[:, t, c0:c0 + w], ps, ALU.add, m)
            square(n, t, m)
            return m

        project(I["w_out_2"][0], cgroups((0, 4, 512)), h, store_h)

        nf = U[:, 0:2048]
        m_nf = G.dma(s_m[2], s_mn[2], lambda e: e.dma_start(nf, I["norm_ffn_2"][0, :].partition_broadcast(128)),
                     T.now(), A.now(), V.now())
        begin(I["peer_w_query_2"][0], [(0, 512)])
        mn = row_norm(False, copied=False)
        hn = P[:, 1, 0:2048], P[:, 1, 2048:4096]
        for t in (1, 0):
            mh = stt(hn[t], x[:, t, :], q1[:, t:t + 1], nf, ALU.mult, ALU.mult, mn, m_nf, T.now())
        ev = lambda k, o, ps, *mk: act(o, ps, ACT.Copy, *mk)
        h = to_h(lambda t, k: hn[t][:, k * 128:(k + 1) * 128], [mh], ev)
        parts = []
        qT = TAB[:, 0:4096].rearrange("p (b n) -> p b n", b=16)
        pieces = [(g, pc) for g in range(4) for pc in range(8)]
        for q, (g, pc) in enumerate(pieces):
            while asked[0] < min(q + NB, len(pieces)):
                ahead.append(split(I["peer_w_query_2"][0], 512 * pieces[asked[0]][0], 512, pieces[asked[0]][1]))
                asked[0] += 1
            raw, hi, lo, m, ml, i, j = ahead.pop(0)
            if g == 0:
                if pc == 0:
                    parts += [next(h), next(h), next(h)]
                if pc == 2:
                    parts.append(next(h))
                    tpn[0] += 1
                ready_h = parts[pc // 2]
            if pc == 0:
                pr, pi = pair()
            for b in range(4):
                for k in range(2):
                    kk = pc * 2 + k
                    ws = hi[:, k, b * 128:(b + 1) * 128], lo[:, k, b * 128:(b + 1) * 128]
                    fin = three(pr[:, b * 256:(b + 1) * 256], ws, (hH[:, kk, :], hL[:, kk, :]),
                                kk == 0 and b % 2 == 0, kk == 15, ml, ready_h, skip=True, last=(k == 1))
            w_free[j] = fin
            if pc == 7:
                tp_free[pi] = [act(qT[:, 4 * g:4 * g + 4, :], pr[:, :].rearrange("p (b n) -> p b n", b=4), ACT.Copy, fin)]
        skT = S[:, 0:2048]
        for b0 in (0, 8):
            sk, m, i = load(I["peer_sub_keys_2"][0].rearrange("h s n c -> n (h s) c")[:, b0:b0 + 8, :], (8, 128))
            pr, pi = pair()
            for b in range(8):
                mt = tr(pr[:, b * 128:(b + 1) * 128], sk[:, b, :], m, last=True)
            tp_free[pi] = [vcopy(skT[:, b0 * 128:(b0 + 8) * 128], pr[:, :], mt, RX.act)]
            r_free[i] = [mt]
        msk = V.now()

        hx = P[:, 0, 0:4352]
        oh = hx[:, 0:2048].rearrange("p (h k a) -> p h k a", h=8, k=16)
        tv = hx[:, 2048:2304].rearrange("p (b k) -> p b k", b=16)
        ti = hx[:, 2304:2560].bitcast(U32).rearrange("p (b k) -> p b k", b=16)
        tf = hx[:, 2560:2816].rearrange("p (b k) -> p b k", b=16)
        bv = hx[:, 2816:2944].rearrange("p (h k) -> p h k", h=8)
        bj = hx[:, 2944:3072].bitcast(U32)
        bh = hx[:, 3072:3200].bitcast(U32)
        fa = hx[:, 3200:3328]
        fi = [hx[:, 3328:3456], hx[:, 3456:3584]]
        aa = hx[:, 3584:3840].rearrange("p (t j) -> p t j", t=2)
        co = hx[:, 3840:4096].rearrange("p (t j) -> p t j", t=2)
        ix = hx[:, 4096:4352].bitcast(U32).rearrange("p (t j) -> p t j", t=2)
        sc = U[:, 0:2048]
        ca = U[:, 2048:4096]
        V.wait(T.now(), A.now())

        def scores(t):
            for b0 in (0, 8):
                pr, i = pair()
                for b in range(8):
                    m = mm(pr[:, b * 128:(b + 1) * 128], qT[:, b0 + b, t * 128:(t + 1) * 128],
                           skT[:, (b0 + b) * 128:(b0 + b + 1) * 128], True, True, msk, A.now(), last=(b == 7))
                tp_free[i] = [act(sc[:, b0 * 128:(b0 + 8) * 128], pr[:, :], ACT.Copy, m, V.now())]

        def top16(src, val, idx):
            V.then(lambda e: e.max(val[:, 0:8], src), A.now())
            V.then(lambda e: e.max_index(idx[:, 0:8], val[:, 0:8], src))
            V.then(lambda e: e.match_replace(src, val[:, 0:8], src, TAKEN))
            V.then(lambda e: e.max(val[:, 8:16], src))
            V.then(lambda e: e.max_index(idx[:, 8:16], val[:, 8:16], src))

        def choose(t, h0):
            for b in range(2 * h0, 2 * h0 + 4):
                top16(sc[:, b * 128:(b + 1) * 128], tv[:, b, :], ti[:, b, :])
                yield
            h2 = slice(h0, h0 + 2)
            j2 = slice(h0 * 16, h0 * 16 + 32)
            vcopy(tf[:, 2 * h0:2 * h0 + 4, :], ti[:, 2 * h0:2 * h0 + 4, :])
            t0 = tv.rearrange("p (h s) k -> p h s k", s=2)
            f0 = tf.rearrange("p (h s) k -> p h s k", s=2)
            c4 = ca.rearrange("p (h a b) -> p h a b", h=8, a=16)
            tt(c4[:, h2, :, :], t0[:, h2, 0, :].unsqueeze(3).to_broadcast([128, 2, 16, 16]),
               t0[:, h2, 1, :].unsqueeze(2).to_broadcast([128, 2, 16, 16]), ALU.add)
            bj8 = bj.rearrange("p (h k) -> p h k", h=8)
            yield
            for h in range(h0, h0 + 2):
                top16(ca[:, h * 256:(h + 1) * 256], bv[:, h, :], bj8[:, h, :])
                yield
            io = CW[:, INV + 64:INV + 80]
            for s in range(2):
                if s == 0:
                    V.then(lambda e: e.tensor_scalar(bh[:, j2], bj[:, j2], 4, None, ALU.logical_shift_right))
                else:
                    V.then(lambda e: e.tensor_scalar(bh[:, j2], bj[:, j2], 15, None, ALU.bitwise_and))
                vcopy(fa[:, j2], bh[:, j2])
                for h in range(h0, h0 + 2):
                    fh = fa[:, h * 16:(h + 1) * 16].unsqueeze(2).to_broadcast([128, 16, 16])
                    V.do(lambda e, h=h, fh=fh: e.tensor_tensor(oh[:, h, :, :], fh, io.unsqueeze(1).to_broadcast([128, 16, 16]),
                                                               ALU.is_equal), V.now() if h == h0 else None)
                tt(oh[:, h2, :, :], oh[:, h2, :, :], f0[:, h2, s, :].unsqueeze(2).to_broadcast([128, 2, 16, 16]), ALU.mult)
                red(fi[s].rearrange("p (h k) -> p h k", h=8)[:, h2, :], oh[:, h2, :, :], ALU.add)
                yield
            stt(fa[:, j2], fi[0][:, j2], 128.0, fi[1][:, j2], ALU.mult, ALU.add)
            mi[t, h0] = vcopy(ix[:, t, j2], fa[:, j2])
            c3 = co[:, t, :].rearrange("p (h k) -> p h k", h=8)[:, h2, :]
            m = tt(c3, bv[:, h2, :], bv[:, h2, 0:1].to_broadcast([128, 2, 16]), ALU.subtract)
            m = act(c3, c3, ACT.Exp, m)
            red(ss[:, 0:2], c3, ALU.add, m)
            recip(ss[:, 0:2], ss[:, 0:2])
            tt(c3, c3, ss[:, 0:2].unsqueeze(2).to_broadcast([128, 2, 16]), ALU.mult)
            yield


        rf = ring[:, :, :].rearrange("p s n -> p (s n)")
        gs = [rf[:, 0:2048], rf[:, 2048:4096], P[:, 0, 4400:6448], P[:, 1, 4096:6144], SY[:, 0:2048],
              TAB[:, 0:2048], TAB[:, 2048:4096], S[:, 0:2048]]
        g_sem = [sem(f"s_g{j}") for j in range(8)]
        g_cnt = [[0] for _ in range(8)]
        g_free = [None] * 8
        g_order = [0, 1, 2, 3, 4]

        def gather(tab, t, j, mi):
            i = g_order.pop(0)
            g_order.append(i)
            return gs[i], G.dma(g_sem[i], g_cnt[i], lambda e: e.indirect_dma_start(
                gs[i], None, tab[0], bass.IndirectOffsetOnAxis(ap=ix[:, t, j:j + 1], axis=0)), mi, g_free[i]), i

        def dots(t, j0, between):
            for j in range(j0, j0 + 32):
                u, m, i = gather(I["peer_u_2"], t, j, mi[t, j0 // 16])
                g_free[i] = V.then(lambda e, u=u, j=j: e.tensor_tensor_reduce(
                    out=u, in0=u, in1=hn[t], scale=1.0, scalar=0.0, op0=ALU.mult, op1=ALU.add,
                    accum_out=aa[:, t, j:j + 1]), m)
                if between:
                    pump((0.34, 0, 0))

        def mix(t):
            for j in range(128):
                v, m, i = gather(I["peer_v_2"], t, j, None)
                g_free[i] = V.then(lambda e, v=v, j=j: e.scalar_tensor_tensor(
                    out=x[:, t, :], in0=v, scalar=co[:, t, j:j + 1], in1=x[:, t, :], op0=ALU.mult, op1=ALU.add), m)

        mi = {}
        G.wait(T.now(), V.now(), A.now())
        scores(0)
        todo.append(choose(0, 0))
        drain(todo)
        for t in range(2):
            for h0 in range(0, 8, 2):
                if (t, h0) != (1, 6):
                    if h0 == 6:
                        scores(1)
                        for j in (5, 6, 7):
                            g_free[j] = T.now()
                            g_order.append(j)
                    todo.append(choose(*((t, h0 + 2) if h0 < 6 else (1, 0))))
                dots(t, 16 * h0, True)
                drain(todo)
        for t in range(2):
            m = act(aa[:, t, :], aa[:, t, :], ACT.Gelu, V.now())
            tt(co[:, t, :], co[:, t, :], aa[:, t, :], ALU.mult, m)
        o_d = out.rearrange("a (t p) d -> (a p) t d", p=128)
        for t in range(2):
            mix(t)
            m = S_.dma(s_o, s_on, lambda e, t=t: e.dma_start(o_d[:, t, :], x[:, t, :]), V.now())
        S_.wait(m)

        block = ctx.enter_context(nc.Block())
        for lane, deco in ((S_, block.sync), (A, block.scalar), (V, block.vector), (G, block.gpsimd), (T, block.tensor)):
            def run(e, lane=lane):
                for f in lane.q:
                    f(e)
            deco(run)


_INS = ["x", "c", "positions", "rel_bias", "norm_gain", "w_mod", "b_mod", "w_in", "q_norm_gain", "k_norm_gain",
        "ret_norm_gain", "w_out", "meta_tokens_2", "norm_mix_2", "w_in_2", "b_forget_2", "fox_q_gain_2",
        "fox_k_gain_2", "sb_out_gain_2", "fox_out_gain_2", "w_out_2", "norm_ffn_2", "peer_w_query_2",
        "peer_sub_keys_2", "peer_u_2", "peer_v_2"]


def kernel(**inputs):
    import concourse.bacc as _bacc
    from concourse import mybir as _mybir
    from concourse.bass_utils import run_bass_kernel_spmd as _run

    nc = _bacc.Bacc("TRN2", target_bir_lowering=False, num_devices=1)
    arrays, args = {}, {}
    cw, dm = constants()
    given = {name: np.ascontiguousarray(inputs[name]) for name in _INS}
    given["cw"], given["dm"] = cw, dm
    for name, a in given.items():
        arrays[f"in_{name}"] = a
        args[name] = nc.dram_tensor(f"in_{name}", a.shape, _mybir.dt.from_np(a.dtype), kind="ExternalInput").ap()
    o = nc.dram_tensor("out_0", (1, 256, 2048), F32, kind="ExternalOutput").ap()
    mixer_peer_program(nc, args, o)
    r = _run(nc, [arrays], core_ids=[0])
    return r.results[0]["out_0"]
```
